# Optimizing a Trainium2 kernel written in Bass

```python
import math
import jax, jax.numpy as jnp
from jax import lax
import numpy as np

D_MODEL = 1024
BATCH = 1
SEQ = 256
DEPTH = 2

GRID_W = 64
CTX_LEN = 256

N_ATTN_LAYERS = (DEPTH + 1) // 2
N_SSM_LAYERS = DEPTH // 2

ATTN_WIDTH = D_MODEL // 2
HEAD_DIM = 64
N_Q_HEADS = ATTN_WIDTH // HEAD_DIM
N_KV_HEADS = 2
Q_PER_KV = N_Q_HEADS // N_KV_HEADS
KV_WIDTH = N_KV_HEADS * HEAD_DIM
Q_BLOCK = 128
ROPE_THETA = 10000.0
GMLP_WIDTH = D_MODEL // 2
GMLP_CHUNK = 128
GMLP_GROUPS = 4
GMLP_GROUP_DIM = GMLP_WIDTH // GMLP_GROUPS
MIX_IN = ATTN_WIDTH + 2 * KV_WIDTH + 2 * GMLP_WIDTH
MIX_OUT = ATTN_WIDTH + GMLP_WIDTH
SSM_INNER = 2 * D_MODEL
SSM_HEAD_DIM = 64
SSM_HEADS = SSM_INNER // SSM_HEAD_DIM
SSM_GROUPS = 4
SSM_STATE = 128
SSM_CONV = 3
SSM_CHUNK = 128
SSM_BC_WIDTH = SSM_GROUPS * SSM_STATE
SSM_CONV_DIM = SSM_INNER + 2 * SSM_BC_WIDTH
SSM_IN = SSM_INNER + SSM_CONV_DIM + 2 * SSM_HEADS
FFN_HIDDEN = -(-8 * D_MODEL // (3 * 256)) * 256
NORM_EPS = 1e-6

kernel_name = "hybrid_dit_gmlp_gqa_ssd_block"

def rms_norm(x, g):
    xf = x.astype(jnp.float32)
    y = xf * lax.rsqrt(jnp.mean(xf * xf, axis=-1, keepdims=True) + NORM_EPS)
    return (y * g.astype(jnp.float32)).astype(x.dtype)

def adaln(cond, w, b):
    return jnp.split(jax.nn.silu(cond) @ w + b, 6, axis=-1)

def modulate(h, shift, scale):
    return h * (1 + scale) + shift

def axial_rope_tables(rows):
    t = jnp.arange(rows * GRID_W)
    row = (t // GRID_W).astype(jnp.float32)
    col = (t % GRID_W).astype(jnp.float32)
    n_freq = HEAD_DIM // 4
    inv = ROPE_THETA ** (-jnp.arange(n_freq, dtype=jnp.float32) / n_freq)
    ang = jnp.concatenate([row[:, None] * inv, col[:, None] * inv], axis=-1)
    return jnp.cos(ang), jnp.sin(ang)

def apply_rope(x, cos, sin):
    half = HEAD_DIM // 2
    x1 = x[..., :half].astype(jnp.float32)
    x2 = x[..., half:].astype(jnp.float32)
    cs = cos[None, :, None, :]
    sn = sin[None, :, None, :]
    return jnp.concatenate([x1 * cs - x2 * sn, x2 * cs + x1 * sn], axis=-1).astype(x.dtype)

def gqa_attend(q, k, v):
    s = jnp.einsum("bqkgd,btkd->bkgqt", q, k).astype(jnp.float32) * (HEAD_DIM ** -0.5)
    p = jax.nn.softmax(s, axis=-1).astype(v.dtype)
    return jnp.einsum("bkgqt,btkd->bqkgd", p, v)

def latent_attention(q, k, v, k_ctx, v_ctx):
    b, s = q.shape[:2]
    k_all = jnp.concatenate([k_ctx, k], axis=1)
    v_all = jnp.concatenate([v_ctx, v], axis=1)
    qb = q.reshape(b, s // Q_BLOCK, Q_BLOCK, N_KV_HEADS, Q_PER_KV, HEAD_DIM).transpose(1, 0, 2, 3, 4, 5)
    o = lax.map(lambda qi: gqa_attend(qi, k_all, v_all), qb)
    return o.transpose(1, 0, 2, 3, 4, 5).reshape(b, s, ATTN_WIDTH)

def spatial_gating(u, v, norm_g, w_s, b_s):
    b, l, _ = u.shape
    vn = rms_norm(v.reshape(b, l, GMLP_GROUPS, GMLP_GROUP_DIM), norm_g.reshape(GMLP_GROUPS, GMLP_GROUP_DIM))
    vc = vn.reshape(b, l // GMLP_CHUNK, GMLP_CHUNK, GMLP_GROUPS, GMLP_GROUP_DIM)
    s = jnp.einsum("gpq,bnqgc->bnpgc", w_s, vc) + b_s.T[None, None, :, :, None]
    return u * s.reshape(b, l, GMLP_WIDTH)

def attn_gmlp_mixer(hx, hc, w_in, w_out, q_g, k_g, sgu_g, sgu_w, sgu_b, cos, sin):
    def project(h):
        b, l = h.shape[:2]
        p = h @ w_in
        q, k, v, gm = jnp.split(p, [ATTN_WIDTH, ATTN_WIDTH + KV_WIDTH, ATTN_WIDTH + 2 * KV_WIDTH], axis=-1)
        q = rms_norm(q.reshape(b, l, N_Q_HEADS, HEAD_DIM), q_g)
        k = rms_norm(k.reshape(b, l, N_KV_HEADS, HEAD_DIM), k_g)
        v = v.reshape(b, l, N_KV_HEADS, HEAD_DIM)
        gu, gv = jnp.split(jax.nn.gelu(gm), 2, axis=-1)
        return q, k, v, gu, gv

    b, l = hx.shape[:2]
    lc = hc.shape[1]
    qx, kx, vx, ux, gx = project(hx)
    qc, kc, vc, uc, gc = project(hc)
    qx = apply_rope(qx, cos, sin)
    kx = apply_rope(kx, cos, sin)
    att_x = latent_attention(qx.reshape(b, l, N_KV_HEADS, Q_PER_KV, HEAD_DIM), kx, vx, kc, vc)
    att_c = gqa_attend(qc.reshape(b, lc, N_KV_HEADS, Q_PER_KV, HEAD_DIM), kc, vc).reshape(b, lc, ATTN_WIDTH)
    sg_x = spatial_gating(ux, gx, sgu_g, sgu_w, sgu_b)
    sg_c = spatial_gating(uc, gc, sgu_g, sgu_w, sgu_b)
    out_x = jnp.concatenate([att_x, sg_x], axis=-1) @ w_out
    out_c = jnp.concatenate([att_c, sg_c], axis=-1) @ w_out
    return out_x, out_c

def depthwise_conv(x, w, b):
    k = w.shape[0]
    y = lax.conv_general_dilated(x, w[:, None, :].astype(x.dtype), window_strides=(1,),
                                 padding=[((k - 1) // 2, k // 2)],
                                 dimension_numbers=("NWC", "WIO", "NWC"),
                                 feature_group_count=x.shape[-1])
    return y + b

def ssd_scan(x, dt, a, bm, cm, h0):
    b, l, h, p = x.shape
    g, n = bm.shape[2], bm.shape[3]
    r = h // g
    nc = l // SSM_CHUNK
    L = SSM_CHUNK
    xd = (x * dt[..., None]).reshape(b, nc, L, g, r, p)
    da = (dt * a).reshape(b, nc, L, g, r).transpose(0, 3, 4, 1, 2)
    bc = bm.reshape(b, nc, L, g, n)
    cc = cm.reshape(b, nc, L, g, n)
    a_cs = jnp.cumsum(da, axis=-1)
    lower = jnp.tril(jnp.ones((L, L), dtype=bool))
    seg = jnp.where(lower, a_cs[..., :, None] - a_cs[..., None, :], -jnp.inf)
    decay_in = jnp.exp(seg)
    cb = jnp.einsum("bclgn,bcsgn->bgcls", cc, bc)
    y_diag = jnp.einsum("bgcls,bgrcls,bcsgrp->bclgrp", cb, decay_in, xd)
    decay_to_end = jnp.exp(a_cs[..., -1:] - a_cs)
    chunk_states = jnp.einsum("bcsgn,bgrcs,bcsgrp->cbgrpn", bc, decay_to_end, xd)
    chunk_decay = jnp.exp(a_cs[..., -1]).transpose(3, 0, 1, 2)

    def step(state, inp):
        s_c, dec = inp
        return state * dec[..., None, None] + s_c, state

    h_final, h_start = lax.scan(step, h0.reshape(b, g, r, p, n), (chunk_states, chunk_decay))
    y_off = jnp.einsum("bclgn,cbgrpn,bgrcl->bclgrp", cc, h_start, jnp.exp(a_cs))
    y = (y_diag + y_off).reshape(b, l, h, p)
    return y, h_final.reshape(b, h, p, n)

def maybe_flip(t, rev):
    return jnp.flip(t, axis=1) if rev else t

def ssd_mixer(hx, hc, w_in, conv_w, conv_b, dt_bias, a_log, d_skip, norm_g, w_out):
    a = -jnp.exp(a_log.astype(jnp.float32))

    def prep(h):
        b, l = h.shape[:2]
        p = h @ w_in
        z, xbc, dt = jnp.split(p, [SSM_INNER, SSM_INNER + SSM_CONV_DIM], axis=-1)
        xbc = jax.nn.silu(depthwise_conv(xbc, conv_w, conv_b))
        xs, bm, cm = jnp.split(xbc, [SSM_INNER, SSM_INNER + SSM_BC_WIDTH], axis=-1)
        xs = xs.reshape(b, l, SSM_HEADS, SSM_HEAD_DIM).astype(jnp.float32)
        bm = bm.reshape(b, l, SSM_GROUPS, SSM_STATE).astype(jnp.float32)
        cm = cm.reshape(b, l, SSM_GROUPS, SSM_STATE).astype(jnp.float32)
        dt = jax.nn.softplus(dt.astype(jnp.float32).reshape(b, l, 2, SSM_HEADS) + dt_bias.astype(jnp.float32))
        return z, xs, bm, cm, dt

    zx, xx, bx, cx, dtx = prep(hx)
    zc, xc, bc, cc, dtc = prep(hc)
    b = hx.shape[0]
    d = d_skip.astype(jnp.float32)[:, None]
    y_x = d * xx
    y_c = d * xc
    for direction in range(2):
        rev = direction == 1
        h0 = jnp.zeros((b, SSM_HEADS, SSM_HEAD_DIM, SSM_STATE), jnp.float32)
        yc_d, hc_d = ssd_scan(maybe_flip(xc, rev), maybe_flip(dtc[:, :, direction], rev), a[direction],
                              maybe_flip(bc, rev), maybe_flip(cc, rev), h0)
        yx_d, _ = ssd_scan(maybe_flip(xx, rev), maybe_flip(dtx[:, :, direction], rev), a[direction],
                           maybe_flip(bx, rev), maybe_flip(cx, rev), hc_d)
        y_c = y_c + maybe_flip(yc_d, rev)
        y_x = y_x + maybe_flip(yx_d, rev)

    def finish(y, z):
        b_, l_ = z.shape[:2]
        y = y.reshape(b_, l_, SSM_INNER) * jax.nn.silu(z.astype(jnp.float32))
        y = rms_norm(y.reshape(b_, l_, SSM_GROUPS, SSM_INNER // SSM_GROUPS),
                     norm_g.reshape(SSM_GROUPS, SSM_INNER // SSM_GROUPS)).reshape(b_, l_, SSM_INNER)
        return y.astype(z.dtype) @ w_out

    return finish(y_x, zx), finish(y_c, zc)

def swiglu(h, w_in, w_out):
    g, u = jnp.split(h @ w_in, 2, axis=-1)
    return (jax.nn.silu(g) * u) @ w_out

def setup_inputs(seed: int = 0) -> dict:
    key = jax.random.key(seed)
    ks = jax.random.split(key, 28)
    f32 = jnp.float32

    def nrm(k, shape, fan_in):
        return jax.random.normal(k, shape, f32) * fan_in ** -0.5

    def gain(k, shape):
        return 1.0 + 0.05 * jax.random.normal(k, shape, f32)

    dt0 = jnp.exp(jax.random.uniform(ks[22], (N_SSM_LAYERS, 2, SSM_HEADS), f32, math.log(1e-3), math.log(1e-1)))
    return {
        "x": jax.random.normal(ks[0], (BATCH, SEQ, D_MODEL), f32),
        "c": jax.random.normal(ks[1], (BATCH, D_MODEL), f32),
        "ctx": jax.random.normal(ks[2], (BATCH, CTX_LEN, D_MODEL), f32),
        "c_ctx": jax.random.normal(ks[3], (D_MODEL,), f32),
        "ada_w": nrm(ks[4], (DEPTH, D_MODEL, 6 * D_MODEL), D_MODEL),
        "ada_b": 0.02 * jax.random.normal(ks[5], (DEPTH, 6 * D_MODEL), f32),
        "norm1_g": gain(ks[6], (DEPTH, D_MODEL)),
        "norm2_g": gain(ks[7], (DEPTH, D_MODEL)),
        "ffn_w_in": nrm(ks[8], (DEPTH, D_MODEL, 2 * FFN_HIDDEN), D_MODEL),
        "ffn_w_out": nrm(ks[9], (DEPTH, FFN_HIDDEN, D_MODEL), FFN_HIDDEN),
        "mix_w_in": nrm(ks[10], (N_ATTN_LAYERS, D_MODEL, MIX_IN), D_MODEL),
        "mix_w_out": nrm(ks[11], (N_ATTN_LAYERS, MIX_OUT, D_MODEL), MIX_OUT),
        "q_norm_g": gain(ks[12], (N_ATTN_LAYERS, HEAD_DIM)),
        "k_norm_g": gain(ks[13], (N_ATTN_LAYERS, HEAD_DIM)),
        "sgu_norm_g": gain(ks[14], (N_ATTN_LAYERS, GMLP_WIDTH)),
        "sgu_w": nrm(ks[15], (N_ATTN_LAYERS, GMLP_GROUPS, GMLP_CHUNK, GMLP_CHUNK), GMLP_CHUNK),
        "sgu_b": gain(ks[16], (N_ATTN_LAYERS, GMLP_GROUPS, GMLP_CHUNK)),
        "ssm_w_in": nrm(ks[17], (N_SSM_LAYERS, D_MODEL, SSM_IN), D_MODEL),
        "ssm_conv_w": nrm(ks[18], (N_SSM_LAYERS, SSM_CONV, SSM_CONV_DIM), SSM_CONV),
        "ssm_conv_b": 0.02 * jax.random.normal(ks[19], (N_SSM_LAYERS, SSM_CONV_DIM), f32),
        "ssm_dt_bias": dt0 + jnp.log(-jnp.expm1(-dt0)),
        "ssm_a_log": jnp.log(jax.random.uniform(ks[20], (N_SSM_LAYERS, 2, SSM_HEADS), f32, 1.0, 16.0)),
        "ssm_d": gain(ks[21], (N_SSM_LAYERS, SSM_HEADS)),
        "ssm_norm_g": gain(ks[23], (N_SSM_LAYERS, SSM_INNER)),
        "ssm_w_out": nrm(ks[24], (N_SSM_LAYERS, SSM_INNER, D_MODEL), SSM_INNER),
    }

def reference(x, c, ctx, c_ctx, ada_w, ada_b, norm1_g, norm2_g, ffn_w_in, ffn_w_out,
              mix_w_in, mix_w_out, q_norm_g, k_norm_g, sgu_norm_g, sgu_w, sgu_b,
              ssm_w_in, ssm_conv_w, ssm_conv_b, ssm_dt_bias, ssm_a_log, ssm_d, ssm_norm_g, ssm_w_out):
    rows = x.shape[1] // GRID_W
    cos, sin = axial_rope_tables(rows)
    h_ctx = ctx
    cond_x = c[:, None, :]
    cond_c = c_ctx[None, None, :]
    for i in range(DEPTH):
        last = i == DEPTH - 1
        mx = adaln(cond_x, ada_w[i], ada_b[i])
        mc = adaln(cond_c, ada_w[i], ada_b[i])
        hx = modulate(rms_norm(x, norm1_g[i]), mx[0], mx[1])
        hc = modulate(rms_norm(h_ctx, norm1_g[i]), mc[0], mc[1])
        j = i // 2
        if i % 2 == 0:
            ox, oc = attn_gmlp_mixer(hx, hc, mix_w_in[j], mix_w_out[j], q_norm_g[j], k_norm_g[j],
                                     sgu_norm_g[j], sgu_w[j], sgu_b[j], cos, sin)
        else:
            ox, oc = ssd_mixer(hx, hc, ssm_w_in[j], ssm_conv_w[j], ssm_conv_b[j], ssm_dt_bias[j],
                               ssm_a_log[j], ssm_d[j], ssm_norm_g[j], ssm_w_out[j])
        x = x + mx[2] * ox
        x = x + mx[5] * swiglu(modulate(rms_norm(x, norm2_g[i]), mx[3], mx[4]), ffn_w_in[i], ffn_w_out[i])
        if not last:
            h_ctx = h_ctx + mc[2] * oc
            h_ctx = h_ctx + mc[5] * swiglu(modulate(rms_norm(h_ctx, norm2_g[i]), mc[3], mc[4]), ffn_w_in[i], ffn_w_out[i])
    return x


_drawn_inputs = setup_inputs


def setup_inputs(seed=0):
    import zlib

    import numpy as np

    out = dict(_drawn_inputs(seed))
    spreads = {}
    factors = {'q_norm_g': 8.0,
     'k_norm_g': 8.0,
     'sgu_norm_g': 2.804,
     'sgu_b': 2.789,
     'ssm_conv_b': 6.42,
     'ssm_d': 8.0}
    for name, (base, spread) in spreads.items():
        noise = np.random.default_rng([zlib.crc32(name.encode()), seed]).standard_normal(out[name].shape)
        drawn = base * np.exp(spread * noise) if base else spread * noise
        out[name] = __import__('jax').numpy.asarray(drawn.astype(out[name].dtype))
    for name, factor in factors.items():
        out[name] = (out[name] * factor).astype(out[name].dtype)
    return out
```

```python
from contextlib import ExitStack

import numpy as np

import concourse.bass as bass
from concourse import mybir

F32 = mybir.dt.float32
F32R = mybir.dt.float32r
ALU = mybir.AluOpType
ACT = mybir.ActivationFunctionType
AX_X = mybir.AxisListType.X

P = 128
D = 1024
KT = D // P
NCTX = 256
NLAT = 256
T = NCTX + NLAT
CTX, LAT, ALL = slice(0, NCTX), slice(NCTX, T), slice(0, T)
HALVES = (CTX, LAT)
FFN = 2816
FT = FFN // P
HD = 64
GROUPS = 4
INNER = 2048
ZT = INNER // P
HPG = 8
GW = HPG * HD
NDT = 64
EPS = 1e-6
CW = KT * P
RING = 4

C_IN0 = 0
N_IN0 = 14
C_OUT0 = C_IN0 + N_IN0
C_FI0 = C_OUT0 + KT
C_FO0 = C_FI0 + 2 * FT
C_IN1 = C_FO0 + 4 * KT
N_IN1 = 41
C_OUT1 = C_IN1 + N_IN1
C_FI1 = C_OUT1 + 2 * KT
C_FO1 = C_FI1 + 2 * FT
C_END = C_FO1 + 4 * KT
FO_KT = (6, 6, 5, 5)
FO_AT = (0, 6, 12, 17)

F_OUT0 = 0
F_FI0 = F_OUT0 + KT
F_FO0 = F_FI0 + FT
F_IN1 = F_FO0 + KT
F_OUT1 = F_IN1 + 25
F_FI1 = F_OUT1 + KT
F_FO1 = F_FI1 + FT

N_UNITS = 10
U_FI0 = 3
U_FO0 = 8

K_ID, K_ONE, K_LE, K_GE, K_GT, K_LT = (i * P for i in range(6))
K_W = 6 * P
PV_COND = 0
PV_ADAB = PV_COND + 2 * KT
PV_G = PV_ADAB + 12 * KT
PV_QG = PV_G + 4 * KT
PV_KG = PV_QG + 1
PV_SG = PV_KG + 1
PV_CW = PV_SG + GROUPS
PV_CB = PV_CW + 72
PV_DTB = PV_CB + 24
PV_YG = PV_DTB + 1
PV_AL = PV_YG + ZT
PV_D = PV_AL + NDT
PV_EPS = PV_D + 32
PV_W = PV_EPS + 1
A_COS, A_SIN, A_ROT, A_BLK, A_SGW, A_SGB = 0, 256, 512, 640, 768, 1280
A_W = 1792

ARENA = 2 * FT * T

ITEMS = {8: [("gv", 0)], 9: [("gv", 1), ("k", 0)], 10: [("gv", 2)], 11: [("gv", 3), ("q", 0)],
         12: [("q", 1)], 13: [("q", 2)], 14: [("q", 3)]}
ORDER = [it for s in sorted(ITEMS) for it in ITEMS[s]]
ROPED = [it for it in ORDER if it[0] != "gv"]
STEPS0 = 17

UNITS = [(qb, kv, i) for qb in range(T // P) for kv in range(2) for i in range(4)]


def key_tiles(qb):
    return 2 if qb < 2 else 4


def at(const, per=0, i=None):
    return const if i is None else const + per * i


def chunk_width(c):
    for base in (C_FO0, C_FO1):
        if base <= c < base + 4 * KT:
            return FO_KT[(c - base) % 4] * P
    return CW


def conv_taps(tile):
    return [PV_CW + tap * 24 + tile for tap in range(3)]


def build(nc, x_in, consts, consts0, pvec, ada_w, w_in0, w_out0, w_fi, w_fo, w_in1, w_out1, out):
    with ExitStack() as ctx:
        def sb(name, shape, dt=F32):
            return ctx.enter_context(nc.sbuf_tensor(name, shape, dt))

        def over(name, region, col, shape, dt=F32):
            return nc.alloc_sbuf_tensor_at(name, shape, dt, offset=region + 4 * col)

        def sem(name):
            return ctx.enter_context(nc.semaphore(name))

        kc = sb("kc", [P, K_W])
        pv = sb("pv", [P, PV_W])
        xT = sb("xT", [P, KT, T])
        whi = sb("whi", [P, RING, CW], F32R)
        silc = sb("silc", [P, 2 * KT])
        mod = sb("mod", [P, 12, KT, 2])
        gain = sb("gain", [P, 4, KT, 2])
        attn_s = sb("attn_s", [P, 4, 4])
        base = (nc.sbuf_base + 31) // 32 * 32
        r_raw = base
        r_h = r_raw + 4 * RING * CW
        r_ada = r_h + 4 * 2 * KT * T
        r_scr = r_ada + 4 * 4 * D
        r_arena = r_scr + 4 * 7 * T
        assert r_arena + 4 * ARENA <= nc.sbuf_usable_end, (r_arena + 4 * ARENA, nc.sbuf_usable_end)

        raw = over("raw", r_raw, 0, [P, RING, CW])
        wlo = over("wlo", r_raw, 0, [P, RING, CW], F32R)
        hhi = over("hhi", r_h, 0, [P, KT, T], F32R)
        hlo = over("hlo", r_h, KT * T, [P, KT, T], F32R)
        aring = over("aring", r_ada, 0, [P, 2, D])
        aacc = over("aacc", r_ada, 2 * D, [P, 2, D])
        scr = over("scr", r_scr, 0, [P, 4, T])
        sqb = over("sqb", r_scr, 4 * T, [P, 2, T])
        sqacc = over("sqacc", r_scr, 6 * T, [P, T])
        ahi = over("ahi", r_arena, 0, [P, FT, T], F32R)
        alo = over("alo", r_arena, FT * T, [P, FT, T], F32R)
        k0 = over("k0", r_arena, ARENA - A_W, [P, A_W])
        ada0 = over("ada0", r_arena, 0, [P, 4, KT, 512])
        cur = [0]

        def arena(name, shape):
            col = cur[0]
            cur[0] += int(np.prod(shape[1:]))
            assert cur[0] <= ARENA, name
            return over(name, r_arena, col, shape)

        qT = arena("qT", [P, 4, T])
        kT = arena("kT", [P, 1, T])
        vT = arena("vT", [P, T])
        uT = arena("uT", [P, GROUPS, T])
        gvT = arena("gvT", [P, GROUPS, T])
        toks = arena("toks", [P, 5, 4, P])
        prob = arena("prob", [P, 3, T])
        probT = arena("probT", [P, 2, 4, 4, P])
        isq = arena("isq", [P, 2, T])
        istd = arena("istd", [P, 2, T])
        irst = arena("irst", [P, 2, T])
        rtmp = arena("rtmp", [P, 2, NLAT])
        assert cur[0] <= ARENA - A_W
        cur[0] = 0
        zT = arena("zT", [P, ZT, NLAT])
        tok = arena("tok", [P, 4, GW + INNER])
        CT = arena("CT", [P, GROUPS, NLAT])
        CBm = arena("CBm", [P, 2, 2, GROUPS, P])
        BT = arena("BT", [P, GROUPS, NLAT])
        dts = arena("dts", [P, 8, 4 * NDT])
        dt_ = arena("dt_", [P, 4, NDT])
        da = arena("da", [P, 4, NDT])
        expa = arena("expa", [P, NDT])
        EX = arena("EX", [P, 384])
        dtW = arena("dtW", [P, 6, 32])
        xs_ = over("xs_", r_h, 0, [P, 2, 5, GW])
        DM = over("DM", r_h, 10 * GW, [P, 4, 4, P])
        Eb = over("Eb", r_h, 14 * GW, [P, 2, 4, P])
        H0 = over("H0", r_ada, 0, [P, 2, GW])
        H1 = over("H1", r_ada, 2 * GW, [P, 2, GW])
        Mb = over("Mb", r_ada, 4 * GW, [P, 4, 4, P])
        yhi = hhi[:, :, :].rearrange("p k (a n) -> p (k a) n", a=2)
        ylo = hlo[:, :, :].rearrange("p k (a n) -> p (k a) n", a=2)
        EXC, EXW, EXD = 0, 128, 320
        SPANS = [(0, 0), (0, 1), (0, 2), (1, 0), (1, 1), (1, 3)]

        bank = [ctx.enter_context(nc.psum_tensor(f"bank{b}", [P, 512], F32)) for b in range(8)]

        ident = kc[:, K_ID:K_ID + P]
        ones = kc[:, K_ONE:K_ONE + P]
        incl = [kc[:, K_LE:K_LE + P], kc[:, K_GE:K_GE + P]]
        strict = [kc[:, K_GT:K_GT + P], kc[:, K_LT:K_LT + P]]
        eps = pv[:, PV_EPS:PV_EPS + 1]

        const_in = sem("const_in")
        x_landed = sem("x_landed")
        ada0_in = [sem(f"ada0_in{i}") for i in range(4)]
        raw_in = [sem(f"raw_in{i}") for i in range(RING)]
        ada_in = [sem(f"ada_in{i}") for i in range(2)]
        hi_ready = sem("hi_ready")
        lo_ready = sem("lo_ready")
        chunk_used = sem("chunk_used")
        cond_silu = sem("cond_silu")
        ada0_sum = sem("ada0_sum")
        ada_used = sem("ada_used")
        ada_sum = sem("ada_sum")
        mods_ready = sem("mods_ready")
        gains_ready = sem("gains_ready")
        squared = sem("squared")
        sq_added = sem("sq_added")
        norm_sum = sem("norm_sum")
        std_ready = sem("std_ready")
        rstd_ready = sem("rstd_ready")
        scaled = sem("scaled")
        hhi_ready = sem("hhi_ready")
        hlo_ready = sem("hlo_ready")
        freed = sem("freed")
        in0_out = sem("in0_out")
        it_sq = sem("it_sq")
        it_sum = sem("it_sum")
        it_std = sem("it_std")
        it_rst = sem("it_rst")
        it_scaled = sem("it_scaled")
        rot_done = sem("rot_done")
        rope_tmp = sem("rope_tmp")
        roped = sem("roped")
        turned = sem("turned")
        toks_ready = sem("toks_ready")
        scores_ready = sem("scores_ready")
        rowmax = sem("rowmax")
        bias_ready = sem("bias_ready")
        exp_done = sem("exp_done")
        recip_done = sem("recip_done")
        probs_ready = sem("probs_ready")
        probs_turned = sem("probs_turned")
        probT_ready = sem("probT_ready")
        pv_done = sem("pv_done")
        att_hi = sem("att_hi")
        att_lo = sem("att_lo")
        spatial = sem("spatial")
        sgu_biased = sem("sgu_biased")
        sgu_full = sem("sgu_full")
        sgu_hi = sem("sgu_hi")
        sgu_lo = sem("sgu_lo")
        silu_ready = sem("silu_ready")
        ahi_ready = sem("ahi_ready")
        alo_ready = sem("alo_ready")
        conv_mid = sem("conv_mid")
        conv_left = sem("conv_left")
        conv_silu = sem("conv_silu")
        conv_turned = sem("conv_turned")
        tok_ready = sem("tok_ready")
        bt_ready = sem("bt_ready")
        dt_biased = sem("dt_biased")
        dt_turned = sem("dt_turned")
        dt_chain = sem("dt_chain")
        dt_exp = sem("dt_exp")
        sums_done = sem("sums_done")
        decays = sem("decays")
        dtw_ready = sem("dtw_ready")
        cb_done = sem("cb_done")
        cbm_ready = sem("cbm_ready")
        z_ready = sem("z_ready")
        x_ready = sem("x_ready")
        dm_ready = sem("dm_ready")
        states = sem("states")
        h0_ready = sem("h0_ready")
        h_decayed = sem("h_decayed")
        h1_ready = sem("h1_ready")
        seg_done = sem("seg_done")
        e_ready = sem("e_ready")
        m_ready = sem("m_ready")
        yoff_done = sem("yoff_done")
        toff_ready = sem("toff_ready")
        ydiag_done = sem("ydiag_done")
        y_part = sem("y_part")
        y_ready = sem("y_ready")
        y_turned = sem("y_turned")
        gated = sem("gated")
        y_sq = sem("y_sq")
        y_sum = sem("y_sum")
        y_std = sem("y_std")
        y_rst = sem("y_rst")
        y_full = sem("y_full")
        y_hi = sem("y_hi")
        y_lo = sem("y_lo")
        stored = sem("stored")

        block = ctx.enter_context(nc.Block())

        @block.sync
        def _(sp):
            sp.dma_start(pv[:, :], pvec).then_inc(const_in, 16)
            sp.dma_start(kc[:, :], consts).then_inc(const_in, 16)
            for n in range(4):
                src = ada_w[1 - n // 2, :, (n % 2) * 512:(n % 2 + 1) * 512].rearrange("(k p) n -> p k n", p=P)
                sp.dma_start(ada0[:, n], src).then_inc(ada0_in[n], 16)
                if n == 0:
                    sp.dma_start(xT[:, :, :], x_in).then_inc(x_landed, 16)
            sp.dma_start(k0[:, :], consts0).then_inc(const_in, 16)

            def load(src, c, per=0, i=None):
                if c >= RING:
                    sp.wait_ge(chunk_used, at(c - RING + 1, per, i))
                w = chunk_width(c)
                sp.dma_start(raw[:, c % RING, 0:w], src).then_inc(raw_in[c % RING], 16)

            def load_ada(a, per=0, i=None):
                if a >= 2:
                    sp.wait_ge(ada_used, at(a - 1, per, i))
                src = ada_w[bass.ds(at(a // KT + 2, per // KT, i), 1), (a % KT) * P:(a % KT + 1) * P, :]
                sp.dma_start(aring[:, a % 2, :], src.rearrange("a p n -> p (a n)")).then_inc(ada_in[a % 2], 16)

            def pick(w, n, per=0, i=None):
                return w[bass.ds(at(n, per, i), 1)].rearrange("a p n -> p (a n)")

            for c in range(N_IN0):
                load(w_in0[c], C_IN0 + c)
                if c == RING - 1:
                    load_ada(0)
                    load_ada(1)
                if RING <= c < RING + 8:
                    load_ada(2 * (c - RING) + 2)
                    load_ada(2 * (c - RING) + 3)
            for t in range(KT):
                load(w_out0[t], C_OUT0 + t)
                if C_OUT0 + t >= 18:
                    load_ada(C_OUT0 + t)
            with sp.Fori(0, 5) as i:
                for k in range(8):
                    load(pick(w_fi, k, 8, i), C_FI0 + k, 8, i)
                    load_ada(C_FI0 + k, 8, i)
            for k in range(40, 44):
                load(w_fi[k], C_FI0 + k)
                load_ada(C_FI0 + k)
            for t in range(KT):
                for k in range(4):
                    c = C_FO0 + 4 * t + k
                    load(w_fo[t, :, FO_AT[k] * P:(FO_AT[k] + FO_KT[k]) * P], c)
                    if C_FO0 + 4 <= c < 84:
                        load_ada(c - 4)
            for k in range(5):
                load(w_in1[k], C_IN1 + k)
            with sp.Fori(0, 9) as i:
                for k in range(4):
                    load(pick(w_in1, 5 + k, 4, i), C_IN1 + 5 + k, 4, i)
            with sp.Fori(0, 4) as i:
                for k in range(4):
                    load(pick(w_out1, k, 4, i), C_OUT1 + k, 4, i)
            with sp.Fori(0, 11) as i:
                for k in range(4):
                    load(pick(w_fi, 2 * FT + k, 4, i), C_FI1 + k, 4, i)
            for t in range(KT):
                for k in range(4):
                    load(w_fo[KT + t, :, FO_AT[k] * P:(FO_AT[k] + FO_KT[k]) * P], C_FO1 + 4 * t + k)
            for t in range(KT):
                sp.wait_ge(freed, F_FO1 + t + 1)
                sp.dma_start(out[t], xT[:, t, LAT]).then_inc(stored, 16)
            sp.wait_ge(stored, 16 * KT)

        @block.scalar
        def _(act):
            def hi(c, per=0, i=None):
                if c >= C_END:
                    return
                act.wait_ge(raw_in[c % RING], at(16 * (c // RING + 1), 16 * per // RING, i))
                if c >= RING:
                    act.wait_ge(chunk_used, at(c - RING + 1, per, i))
                w = chunk_width(c)
                nc.scalar.activation(whi[:, c % RING, 0:w], raw[:, c % RING, 0:w], ACT.Copy).then_inc(hi_ready, 1)

            def square(k, t, per=0, i=None, cols=ALL):
                if t >= 2:
                    act.wait_ge(sq_added, at(9 * k + t, per, i))
                src = xT[:, bass.ds(at(t, per, i), 1), cols].rearrange("p a n -> p (a n)")
                nc.scalar.activation(sqb[:, t % 2, cols], src, ACT.Square).then_inc(squared, 1)

            def norm(k, halves):
                lo_, hi_ = halves[0].start, halves[-1].stop
                act.wait_ge(norm_sum, k + 1)
                nc.scalar.activation(scr[:, 2, lo_:hi_], bank[7][:, lo_:hi_], ACT.Sqrt, bias=eps,
                                     scale=1.0 / D).then_inc(std_ready, 1)
                shift = 6 * (k // 2) + 3 * (k % 2)
                for t in range(KT):
                    act.wait_ge(scaled, KT * k + t + 1)
                    for h in halves:
                        c = 0 if h is CTX else 1
                        last = nc.scalar.activation(hhi[:, t, h], scr[:, t % 2, h], ACT.Identity,
                                                    bias=mod[:, shift, t, c:c + 1])
                    last.then_inc(hhi_ready, 1)

            def ffn_in(l, p, per=0, i=None):
                cbase, fbase = (C_FI0, C_FI1)[l], (F_FI0, F_FI1)[l]
                cols = (ALL, LAT)[l]
                pi = None if i is None else i
                hi(cbase + 2 * p + 2, 2 * per, pi)
                hi(cbase + 2 * p + 3, 2 * per, pi)
                act.wait_ge(chunk_used, at(cbase + 2 * p + 1, 2 * per, pi))
                act.wait_ge(freed, at(fbase + p - 1, per, pi))
                nc.scalar.activation(scr[:, p % 2, cols], bank[2 * (p % 2)][:, cols], ACT.Silu).then_inc(silu_ready, 1)
                act.wait_ge(freed, at(fbase + p + 1, per, pi))
                dst = ahi[:, bass.ds(at(p, per, pi), 1), cols].rearrange("p a n -> p (a n)")
                nc.scalar.activation(dst, scr[:, 2 + p % 2, cols], ACT.Copy).then_inc(ahi_ready, 1)

            act.wait_ge(const_in, 48)
            nc.scalar.activation(silc[:, :], pv[:, PV_COND:PV_COND + 2 * KT], ACT.Silu).then_inc(cond_silu, 1)
            act.wait_ge(x_landed, 16)
            for t in range(KT):
                square(0, t)
            hi(0)
            hi(1)
            norm(0, HALVES)

            n_sq = n_std = 0
            srcs = {"gv": gvT, "k": kT, "q": qT}
            for s in range(STEPS0):
                if s < N_IN0:
                    hi(s + 2)
                    act.wait_ge(chunk_used, s + 1)
                    dst, f = ((gvT[:, s, :], ACT.Gelu_apprx_tanh) if s < 4 else
                              (uT[:, s - 4, :], ACT.Gelu_apprx_tanh) if s < 8 else
                              (kT[:, 0, :], ACT.Copy) if s == 8 else (vT[:, :], ACT.Copy) if s == 9 else
                              (qT[:, s - 10, :], ACT.Copy))
                    nc.scalar.activation(dst, bank[s % 4][:, :], f).then_inc(in0_out, 1)
                for name, j in ITEMS.get(s, []):
                    if n_sq >= 2:
                        act.wait_ge(it_sum, n_sq - 1)
                    act.wait_ge(in0_out, {"gv": j, "k": 8, "q": 10 + j}[name] + 1)
                    nc.scalar.activation(isq[:, n_sq % 2, :], srcs[name][:, j, :], ACT.Square).then_inc(it_sq, 1)
                    n_sq += 1
                for name, j in ITEMS.get(s - 1, []):
                    act.wait_ge(it_sum, n_std + 1)
                    if n_std >= 2:
                        act.wait_ge(it_rst, n_std - 1)
                    nc.scalar.activation(istd[:, n_std % 2, :], bank[5 + n_std % 2][:, :], ACT.Sqrt, bias=eps,
                                         scale=1.0 / (P if name == "gv" else HD)).then_inc(it_std, 1)
                    n_std += 1
            for j in range(5):
                act.wait_ge(turned, j + 1)
                nc.scalar.activation(toks[:, j, :, :].rearrange("p a n -> p (a n)"), bank[2 + j % 2][:, :],
                                     ACT.Copy).then_inc(toks_ready, 1)
            for n in range(38):
                if n < 32:
                    keys = P * key_tiles(UNITS[n][0])
                    act.wait_ge(bias_ready, n + 1)
                    if n >= 3:
                        act.wait_ge(probs_turned, n - 2)
                    nc.scalar.activation(prob[:, n % 3, 0:keys], bank[n % 2][:, 0:keys], ACT.Exp,
                                         bias=attn_s[:, n % 4, 1:2], scale=HD ** -0.5,
                                         accum_out=attn_s[:, n % 4, 2:3]).then_inc(exp_done, 1)
                m = n - 2
                if 0 <= m < 32:
                    grp, i, kt = m // 4, m % 4, key_tiles(UNITS[m][0])
                    act.wait_ge(probs_turned, m + 1)
                    if grp >= 2:
                        act.wait_ge(pv_done, grp - 1)
                    nc.scalar.activation(probT[:, grp % 2, 0:kt, i, :],
                                         bank[2 + m % 2][:, 0:kt * P].rearrange("p (a n) -> p a n", n=P),
                                         ACT.Copy).then_inc(probT_ready, 1)
                if n % 8 == 4 and n >= 12:
                    qb = (n - 12) // 8
                    act.wait_ge(pv_done, 2 * qb + 2)
                    nc.scalar.activation(hhi[:, 0:4, qb * P:(qb + 1) * P],
                                         bank[5 + qb % 2][:, :].rearrange("p (a n) -> p a n", n=P),
                                         ACT.Copy).then_inc(att_hi, 1)
                if n % 8 == 0 and n >= 8:
                    g = n // 8 - 1
                    act.wait_ge(sgu_full, g + 1)
                    nc.scalar.activation(hhi[:, 4 + g, :], uT[:, g, :], ACT.Copy).then_inc(sgu_hi, 1)
            for t in range(KT):
                hi(C_OUT0 + t + 2)
                act.wait_ge(freed, F_OUT0 + t + 1)
                square(1, t)
            norm(1, HALVES)
            with act.Fori(0, 5) as i:
                for p in range(4):
                    ffn_in(0, p, 4, i)
            for p in range(20, FT):
                ffn_in(0, p)
            for t in range(KT):
                for k in range(4):
                    hi(C_FO0 + 4 * t + k + 2)
                act.wait_ge(freed, F_FO0 + t + 1)
                square(2, t)
            norm(2, HALVES)

            def conv(j, e, per=0, i=None):
                hi(C_IN1 + j + 2, per, i)
                act.wait_ge(chunk_used, at(C_IN1 + j + 1, per, i))
                tap = conv_taps(e)[1]
                cols = slice(0, T) if e < 20 else slice(0, NLAT)
                nc.scalar.activation(scr[:, e % 2, cols], bank[j % 4][:, cols], ACT.Identity,
                                     bias=pv[:, bass.ds(at(PV_CB + e, per, i), 1)],
                                     scale=pv[:, bass.ds(at(tap, per, i), 1)]).then_inc(conv_mid, 1)
                act.wait_ge(freed, at(F_IN1 + j + 1, per, i))
                if e >= 2 and e < 20:
                    act.wait_ge(conv_turned, at(e - 1, per, i))
                    if i is None:
                        act.wait_ge(bt_ready, min(e - 1, GROUPS))
                dst = scr[:, 2 + e % 2, :] if e < 20 else CT[:, e - 20, :]
                nc.scalar.activation(dst, scr[:, e % 2, cols], ACT.Silu).then_inc(conv_silu, 1)

            def tok_out(e, per=0, i=None):
                act.wait_ge(conv_turned, at(e + 1, per, i))
                nc.scalar.activation(tok[:, :, bass.ds(at(e * P, P * per, i), P)],
                                     bank[4 + e % 2][:, :].rearrange("p (a n) -> p a n", n=P),
                                     ACT.Copy).then_inc(tok_ready, 1)

            conv(0, 0)
            conv(1, 1)
            tok_out(0)
            hi(C_IN1 + 2 + 2)
            conv(3, 2)
            tok_out(1)
            conv(4, 3)
            tok_out(2)
            act.wait_ge(dt_chain, 1)
            nc.scalar.activation(dts[:, 1, :], dts[:, 0, :], ACT.Abs).then_inc(dt_exp, 1)
            act.wait_ge(dt_exp, 1)
            nc.scalar.activation(dts[:, 2, :], dts[:, 1, :], ACT.Exp, scale=-1.0).then_inc(dt_exp, 1)
            nc.scalar.activation(expa[:, :], pv[:, PV_AL:PV_AL + NDT], ACT.Exp).then_inc(dt_exp, 1)
            act.wait_ge(sums_done, 1)
            nc.scalar.activation(EX[:, :], bank[7][:, 0:384], ACT.Exp).then_inc(decays, 1)
            with act.Fori(0, 4) as i:
                for k in range(4):
                    conv(5 + k, 4 + k, 4, i)
                    tok_out(3 + k, 4, i)
            for k in range(GROUPS):
                conv(21 + k, 20 + k)
                if k == 0:
                    tok_out(19)
            for k in range(ZT):
                hi(C_IN1 + 25 + k + 2)
                act.wait_ge(chunk_used, C_IN1 + 25 + k + 1)
                nc.scalar.activation(zT[:, k, :], bank[(25 + k) % 4][:, 0:NLAT], ACT.Silu).then_inc(z_ready, 1)
            for q in range(8):
                act.wait_ge(states, 2 * q + 1)
                if q >= 2:
                    act.wait_ge(yoff_done, 2 * (q - 2) + 1)
                    act.wait_ge(h_decayed, q - 1)
                nc.scalar.activation(H0[:, q % 2, :], bank[0][:, :], ACT.Copy).then_inc(h0_ready, 1)
                for m in range(4 * q, 4 * q + 4):
                    act.wait_ge(seg_done, m + 1)
                    if m >= 2:
                        act.wait_ge(m_ready, m - 1)
                    nc.scalar.activation(Eb[:, m % 2, :, :].rearrange("p a n -> p (a n)"), bank[2 + m % 2][:, :],
                                         ACT.Exp).then_inc(e_ready, 1)
            for j in range(8):
                act.wait_ge(gated, j + 1)
                if j >= 4:
                    act.wait_ge(y_sum, (j - 4) // 2 + 1)
                nc.scalar.activation(scr[:, j % 4, :], zT[:, 2 * j:2 * j + 2, :].rearrange("p a n -> p (a n)"),
                                     ACT.Square).then_inc(y_sq, 1)
            for g in range(GROUPS):
                act.wait_ge(y_sum, g + 1)
                nc.scalar.activation(sqb[:, g % 2, 0:NLAT], bank[2 + g % 2][:, 0:NLAT], ACT.Sqrt, bias=eps,
                                     scale=1.0 / GW).then_inc(y_std, 1)
                act.wait_ge(y_full, g + 1)
                nc.scalar.activation(yhi[:, 4 * g:4 * g + 4, :], zT[:, 4 * g:4 * g + 4, :], ACT.Copy)\
                    .then_inc(y_hi, 1)
            for t in range(KT):
                hi(C_OUT1 + 2 * t + 2)
                hi(C_OUT1 + 2 * t + 3)
                act.wait_ge(freed, F_OUT1 + t + 1)
                square(3, t, cols=LAT)
            norm(3, (LAT,))
            with act.Fori(0, 5) as i:
                for p in range(4):
                    ffn_in(1, p, 4, i)
            for p in range(20, FT):
                ffn_in(1, p)
            for c in range(C_FO1, C_END):
                hi(c + 2)

        @block.vector
        def _(dve):
            vec = nc.vector

            def lo(c, per=0, i=None):
                if c >= C_END:
                    return
                dve.wait_ge(hi_ready, at(c + 1, per, i))
                w, s = chunk_width(c), c % RING
                vec.tensor_tensor(wlo[:, s, 0:w], raw[:, s, 0:w], whi[:, s, 0:w].bitcast(F32),
                                  ALU.subtract).then_inc(lo_ready, 1)

            def ada_step(a, per=0, i=None):
                k = a % KT
                dve.wait_ge(ada_in[a % 2], at(16 * (a // 2 + 1), 8 * per, i))
                if a:
                    dve.wait_ge(ada_used, at(a, per, i))
                if k == 0 and a:
                    dve.wait_ge(ada_sum, at(a // KT, per // KT, i))
                for c in range(2):
                    col = silc[:, 2 * k + c:2 * k + c + 1]
                    if k == 0:
                        last = vec.tensor_scalar(aacc[:, c, :], aring[:, a % 2, :], col, None, ALU.mult)
                    else:
                        last = vec.scalar_tensor_tensor(out=aacc[:, c, :], in0=aring[:, a % 2, :], scalar=col,
                                                        in1=aacc[:, c, :], op0=ALU.mult, op1=ALU.add)
                last.then_inc(ada_used, 1)

            def add_bias(dst, src, row, per=0, i=None):
                b = pv[:, bass.ds(at(PV_ADAB + row * KT, per * KT, i), KT)]
                b = b.rearrange("p (a n) -> p a n", n=1).broadcast_to([P, KT, 2])
                return vec.tensor_tensor(dst, src, b, ALU.add)

            def ada_finish(u, per=0, i=None):
                dve.wait_ge(ada_sum, at(u + 1, per, i))
                dst = mod[:, bass.ds(at(u + 2, per, i), 1)].rearrange("p a k c -> p (a k) c")
                add_bias(dst, bank[4][:, 0:2 * KT].rearrange("p (k c) -> p k c", c=2), u + 2, per, i)\
                    .then_inc(mods_ready, 1)

            def gains(k, mods):
                dve.wait_ge(mods_ready, mods)
                g = pv[:, PV_G + k * KT:PV_G + (k + 1) * KT].rearrange("p (a n) -> p a n", n=1)
                vec.scalar_tensor_tensor(out=gain[:, k], in0=mod[:, 6 * (k // 2) + 3 * (k % 2) + 1], scalar=1.0,
                                         in1=g.broadcast_to([P, KT, 2]), op0=ALU.add, op1=ALU.mult)\
                    .then_inc(gains_ready, 1)

            def clear_sum(k):
                vec.memset(sqacc[:, :], 0.0).then_inc(sq_added, 1)

            def add_square(k, t, per=0, i=None, cols=ALL):
                dve.wait_ge(squared, at(KT * k + t + 1, per, i))
                dve.wait_ge(sq_added, at(9 * k + t + 1, per, i))
                vec.tensor_tensor(sqacc[:, cols], sqacc[:, cols], sqb[:, t % 2, cols], ALU.add)\
                    .then_inc(sq_added, 1)

            def norm(k, halves):
                lo_, hi_ = halves[0].start, halves[-1].stop
                shift = 6 * (k // 2) + 3 * (k % 2)
                dve.wait_ge(std_ready, k + 1)
                vec.reciprocal(scr[:, 3, lo_:hi_], scr[:, 2, lo_:hi_]).then_inc(rstd_ready, 1)
                dve.wait_ge(rstd_ready, k + 1)
                dve.wait_ge(gains_ready, k + 1)
                for t in range(KT + 1):
                    if t < KT:
                        if t >= 2:
                            dve.wait_ge(hlo_ready, KT * k + t - 1)
                        for h in halves:
                            c = 0 if h is CTX else 1
                            last = vec.scalar_tensor_tensor(out=scr[:, t % 2, h], in0=xT[:, t, h],
                                                            scalar=gain[:, k, t, c:c + 1], in1=scr[:, 3, h],
                                                            op0=ALU.mult, op1=ALU.mult)
                        last.then_inc(scaled, 1)
                    if t >= 1:
                        s = t - 1
                        dve.wait_ge(hhi_ready, KT * k + s + 1)
                        for h in halves:
                            c = 0 if h is CTX else 1
                            last = vec.scalar_tensor_tensor(out=hlo[:, s, h], in0=scr[:, s % 2, h],
                                                            scalar=mod[:, shift, s, c:c + 1],
                                                            in1=hhi[:, s, h].bitcast(F32),
                                                            op0=ALU.add, op1=ALU.subtract)
                        last.then_inc(hlo_ready, 1)

            def residual(row, t, b, halves, psum, per=0, i=None):
                for h in halves:
                    c = 0 if h is CTX else 1
                    xt = xT[:, bass.ds(at(t, per, i), 1), h].rearrange("p a n -> p (a n)")
                    g = mod[:, row, bass.ds(at(t, per, i), 1), c]
                    last = vec.scalar_tensor_tensor(out=xt, in0=bank[b][:, psum(h)], scalar=g, in1=xt,
                                                    op0=ALU.mult, op1=ALU.add)
                last.then_inc(freed, 1)

            def ffn_in(l, p, per=0, i=None):
                cbase, fbase = (C_FI0, C_FI1)[l], (F_FI0, F_FI1)[l]
                cols = (ALL, LAT)[l]
                lo(cbase + 2 * p + 2, 2 * per, i)
                lo(cbase + 2 * p + 3, 2 * per, i)
                if l == 0 and i is not None:
                    ada_step(8 * U_FI0 + 2 * p, 2 * per, i)
                    ada_step(8 * U_FI0 + 2 * p + 1, 2 * per, i)
                dve.wait_ge(chunk_used, at(cbase + 2 * p + 2, 2 * per, i))
                dve.wait_ge(silu_ready, at(FT * l + p + 1, per, i))
                if l or p >= 2 or i is not None:
                    if l or p >= 1:
                        dve.wait_ge(ahi_ready, at(FT * l + p - 1, per, i))
                vec.tensor_tensor(scr[:, 2 + p % 2, cols], scr[:, p % 2, cols], bank[2 * (p % 2) + 1][:, cols],
                                  ALU.mult).then_inc(freed, 1)
                dve.wait_ge(ahi_ready, at(FT * l + p + 1, per, i))
                dst = alo[:, bass.ds(at(p, per, i), 1), cols].rearrange("p a n -> p (a n)")
                src = ahi[:, bass.ds(at(p, per, i), 1), cols].rearrange("p a n -> p (a n)")
                vec.tensor_tensor(dst, scr[:, 2 + p % 2, cols], src.bitcast(F32), ALU.subtract)\
                    .then_inc(alo_ready, 1)

            clear_sum(0)
            for t in range(KT):
                add_square(0, t)
            lo(0)
            lo(1)
            dve.wait_ge(const_in, 48)
            for n, row in enumerate((1, 0)):
                dve.wait_ge(ada0_sum, 2)
                add_bias(mod[:, row], bank[4][:, 32 + 16 * n:48 + 16 * n].rearrange("p (k c) -> p k c", c=2), row)\
                    .then_inc(mods_ready, 1)
            gains(0, 2)
            norm(0, HALVES)

            n_rst = n_rope = 0
            srcs = {"gv": gvT, "k": kT, "q": qT}
            gcol = {"gv": PV_SG, "k": PV_KG, "q": PV_QG}
            done_at = {}
            for s in range(STEPS0):
                if s < N_IN0:
                    lo(s + 2)
                if s < 8:
                    ada_step(2 * s)
                    ada_step(2 * s + 1)
                    if s == 3:
                        ada_finish(0)
                if s == 8:
                    ada_finish(1)
                for name, j in ITEMS.get(s - 1, []):
                    n = n_rst
                    g = gcol[name] + (j if name == "gv" else 0)
                    dve.wait_ge(it_std, n + 1)
                    vec.reciprocal(irst[:, n % 2, :], istd[:, n % 2, :]).then_inc(it_rst, 1)
                    dve.wait_ge(it_rst, n + 1)
                    vec.scalar_tensor_tensor(out=srcs[name][:, j, :], in0=srcs[name][:, j, :],
                                             scalar=pv[:, g:g + 1], in1=irst[:, n % 2, :],
                                             op0=ALU.mult, op1=ALU.mult).then_inc(it_scaled, 1)
                    n_rst += 1
                for name, j in ITEMS.get(s - 2, []):
                    if name == "gv":
                        continue
                    r = n_rope
                    src = srcs[name][:, j, LAT]
                    dve.wait_ge(it_scaled, ORDER.index((name, j)) + 1)
                    if r:
                        dve.wait_ge(roped, r)
                    vec.tensor_tensor(rtmp[:, 0, :], src, k0[:, A_COS:A_COS + NLAT], ALU.mult)
                    dve.wait_ge(rot_done, r + 1)
                    vec.tensor_tensor(rtmp[:, 1, :], bank[7][:, 0:NLAT], k0[:, A_SIN:A_SIN + NLAT], ALU.mult)\
                        .then_inc(rope_tmp, 1)
                    dve.wait_ge(rope_tmp, r + 1)
                    vec.tensor_tensor(src, rtmp[:, 0, :], rtmp[:, 1, :], ALU.add).then_inc(roped, 1)
                    n_rope += 1
            for n in range(38):
                if n < 32:
                    keys = P * key_tiles(UNITS[n][0])
                    dve.wait_ge(scores_ready, n + 1)
                    vec.reduce_max(attn_s[:, n % 4, 0:1], bank[n % 2][:, 0:keys], AX_X).then_inc(rowmax, 1)
                    dve.wait_ge(rowmax, n + 1)
                    vec.tensor_scalar(attn_s[:, n % 4, 1:2], attn_s[:, n % 4, 0:1], -(HD ** -0.5), None, ALU.mult)\
                        .then_inc(bias_ready, 1)
                m = n - 1
                if 0 <= m < 32:
                    keys = P * key_tiles(UNITS[m][0])
                    dve.wait_ge(exp_done, m + 1)
                    vec.reciprocal(attn_s[:, m % 4, 3:4], attn_s[:, m % 4, 2:3]).then_inc(recip_done, 1)
                    dve.wait_ge(recip_done, m + 1)
                    vec.tensor_scalar(prob[:, m % 3, 0:keys], prob[:, m % 3, 0:keys], attn_s[:, m % 4, 3:4], None,
                                      ALU.mult).then_inc(probs_ready, 1)
                if n % 8 == 7 and n < 32:
                    g = n // 8
                    dve.wait_ge(spatial, g + 1)
                    b = k0[:, A_SGB + g * P:A_SGB + (g + 1) * P].rearrange("p (a n) -> p a n", a=1)
                    vec.tensor_tensor(isq[:, 0, :].rearrange("p (a n) -> p a n", n=P),
                                      bank[4][:, :].rearrange("p (a n) -> p a n", n=P),
                                      b.broadcast_to([P, 4, P]), ALU.add).then_inc(sgu_biased, 1)
                    dve.wait_ge(sgu_biased, g + 1)
                    vec.tensor_tensor(uT[:, g, :], uT[:, g, :], isq[:, 0, :], ALU.mult).then_inc(sgu_full, 1)
                if n % 8 == 0 and n >= 8:
                    g = n // 8 - 1
                    dve.wait_ge(sgu_hi, g + 1)
                    vec.tensor_tensor(hlo[:, 4 + g, :], uT[:, g, :], hhi[:, 4 + g, :].bitcast(F32),
                                      ALU.subtract).then_inc(sgu_lo, 1)
                if n % 8 == 4 and n >= 12:
                    qb = (n - 12) // 8
                    dve.wait_ge(att_hi, qb + 1)
                    vec.tensor_tensor(hlo[:, 0:4, qb * P:(qb + 1) * P],
                                      bank[5 + qb % 2][:, :].rearrange("p (a n) -> p a n", n=P),
                                      hhi[:, 0:4, qb * P:(qb + 1) * P].bitcast(F32), ALU.subtract)\
                        .then_inc(att_lo, 1)
            clear_sum(1)
            for t in range(KT):
                lo(C_OUT0 + t + 2)
                ada_step(16 + t)
                dve.wait_ge(chunk_used, C_OUT0 + t + 1)
                dve.wait_ge(mods_ready, 4)
                residual(2, t, t % 2, HALVES, lambda h: h)
                add_square(1, t)
            ada_finish(2)
            gains(1, 5)
            norm(1, HALVES)
            with dve.Fori(0, 5) as i:
                for p in range(4):
                    ffn_in(0, p, 4, i)
                ada_finish(U_FI0, 1, i)
            for p in range(20, FT):
                ffn_in(0, p)
            clear_sum(2)
            dve.wait_ge(mods_ready, 10)
            for t in range(KT):
                for k in range(4):
                    lo(C_FO0 + 4 * t + k + 2)
                    if t < 4:
                        ada_step(8 * U_FO0 + 4 * t + k)
                dve.wait_ge(chunk_used, C_FO0 + 4 * t + 4)
                residual(5, t, t % 2, HALVES, lambda h: h)
                add_square(2, t)
                if t in (1, 3):
                    ada_finish(U_FO0 + t // 2)
            gains(2, 12)
            gains(3, 12)
            norm(2, HALVES)

            def conv(j, e, per=0, i=None):
                lo(C_IN1 + j + 2, per, i)
                segs = 2 if e < 20 else 1
                c = scr[:, e % 2, 0:256 * segs].rearrange("p (a n) -> p a n", a=segs)
                b = bank[j % 4][:, 0:256 * segs].rearrange("p (a n) -> p a n", a=segs)
                left, _, right = conv_taps(e)
                dve.wait_ge(conv_mid, at(e + 1, per, i))
                vec.scalar_tensor_tensor(out=c[:, :, 1:256], in0=b[:, :, 0:255],
                                         scalar=pv[:, bass.ds(at(left, per, i), 1)], in1=c[:, :, 1:256],
                                         op0=ALU.mult, op1=ALU.add).then_inc(conv_left, 1)
                dve.wait_ge(conv_left, at(e + 1, per, i))
                vec.scalar_tensor_tensor(out=c[:, :, 0:255], in0=b[:, :, 1:256],
                                         scalar=pv[:, bass.ds(at(right, per, i), 1)], in1=c[:, :, 0:255],
                                         op0=ALU.mult, op1=ALU.add).then_inc(freed, 1)
                if e < 4:
                    dve.wait_ge(conv_silu, e + 1)
                    vec.tensor_copy(BT[:, e, :], scr[:, 2 + e % 2, LAT]).then_inc(bt_ready, 1)

            conv(0, 0)
            conv(1, 1)
            lo(C_IN1 + 2 + 2)
            dve.wait_ge(chunk_used, C_IN1 + 3)
            vec.tensor_scalar(sqb[:, 0, :], bank[2][:, :], pv[:, PV_DTB:PV_DTB + 1], None, ALU.add)\
                .then_inc(freed, 1)
            conv(3, 2)
            conv(4, 3)
            chain = [0]

            def link(ins):
                chain[0] += 1
                ins.then_inc(dt_chain, 1)
                dve.wait_ge(dt_chain, chain[0])

            V, E, Z, Z2, Q = dts[:, 0, :], dts[:, 2, :], dts[:, 3, :], dts[:, 4, :], dts[:, 5, :]
            dve.wait_ge(dt_turned, 1)
            link(vec.tensor_copy(V.rearrange("p (a n) -> p a n", n=NDT),
                                 bank[6][:, :].rearrange("p (a n) -> p a n", n=P)[:, :, 0:NDT]))
            dve.wait_ge(dt_exp, 3)
            link(vec.tensor_scalar(Q, E, 2.0, None, ALU.add))
            link(vec.reciprocal(Z2, Q))
            link(vec.tensor_tensor(Z, E, Z2, ALU.mult))
            link(vec.tensor_tensor(Z2, Z, Z, ALU.mult))
            link(vec.tensor_scalar(Q, Z2, 1.0 / 17, None, ALU.mult))
            for k in range(7, 0, -1):
                link(vec.scalar_tensor_tensor(out=Q, in0=Q, scalar=1.0 / (2 * k + 1), in1=Z2, op0=ALU.add,
                                              op1=ALU.mult))
            link(vec.scalar_tensor_tensor(out=Q, in0=Q, scalar=1.0, in1=Z, op0=ALU.add, op1=ALU.mult))
            link(vec.tensor_scalar(V, V, 0.0, None, ALU.max))
            link(vec.scalar_tensor_tensor(out=dt_[:, :, :].rearrange("p a n -> p (a n)"), in0=Q, scalar=2.0, in1=V,
                                          op0=ALU.mult, op1=ALU.add))
            link(vec.scalar_tensor_tensor(out=da[:, :, :], in0=dt_[:, :, :], scalar=-1.0,
                                          in1=expa[:, :].rearrange("p (a n) -> p a n", a=1)
                                          .broadcast_to([P, 4, NDT]), op0=ALU.mult, op1=ALU.mult))
            dve.wait_ge(decays, 1)
            for n, (d, tt) in enumerate(SPANS):
                last = vec.tensor_tensor(dtW[:, n, :], dt_[:, tt, 32 * d:32 * d + 32],
                                         EX[:, EXW + 32 * n:EXW + 32 * n + 32], ALU.mult)
            last.then_inc(dtw_ready, 1)
            with dve.Fori(0, 4) as i:
                for k in range(4):
                    conv(5 + k, 4 + k, 4, i)
            for k in range(GROUPS):
                conv(21 + k, 20 + k)
            for k in range(ZT):
                lo(C_IN1 + 25 + k + 2)
                if k == 2:
                    for c2 in range(2):
                        dve.wait_ge(cb_done, c2 + 1)
                        for d in range(2):
                            m = incl[d].rearrange("p (a n) -> p a n", a=1).broadcast_to([P, GROUPS, P])
                            vec.tensor_tensor(CBm[:, d, c2], bank[5 + c2][:, :].rearrange("p (a n) -> p a n", n=P),
                                              m, ALU.mult).then_inc(cbm_ready, 1)

            def per_head(v, n=HD):
                return v.rearrange("p (a n) -> p a n", n=1).broadcast_to([P, v.shape[1], n])

            def heads(v):
                return v.rearrange("p (a n) -> p a n", n=HD)

            def x_of(tt, g):
                return heads(tok[:, tt, GW + g * GW:GW + (g + 1) * GW])

            def prep_x(q):
                g, d = q // 2, q % 2
                if q >= 2:
                    dve.wait_ge(ydiag_done, 4 * (q - 2) + 4)
                    dve.wait_ge(states, 2 * (q - 2) + 2)
                for n in range(3):
                    w = dtW[:, 3 * d + n, g * HPG:(g + 1) * HPG]
                    vec.tensor_tensor(heads(xs_[:, q % 2, n, :]), x_of(SPANS[3 * d + n][1], g), per_head(w), ALU.mult)\
                        .then_inc(x_ready, 1)
                for c2 in range(2):
                    w = dt_[:, 2 + c2, 32 * d + g * HPG:32 * d + (g + 1) * HPG]
                    vec.tensor_tensor(heads(xs_[:, q % 2, 3 + c2, :]), x_of(2 + c2, g), per_head(w), ALU.mult)\
                        .then_inc(x_ready, 1)

            def chunk_of(m):
                q, i = m // 4, m % 4
                return (i // 2) ^ (q % 2), i % 2

            def prep_dm(m):
                q = m // 4
                g, d = q // 2, q % 2
                c2, half = chunk_of(m)
                if m >= 4:
                    dve.wait_ge(seg_done, m - 3)
                h = 32 * d + g * HPG + 4 * half
                vec.tensor_tensor(DM[:, m % 4], incl[d].rearrange("p (a n) -> p a n", a=1).broadcast_to([P, 4, P]),
                                  per_head(da[:, 2 + c2, h:h + 4], P), ALU.mult).then_inc(dm_ready, 1)

            dve.wait_ge(tok_ready, 20)
            dve.wait_ge(dtw_ready, 1)
            dve.wait_ge(chunk_used, C_OUT1)
            prep_x(0)
            for m in range(4):
                prep_dm(m)
            for q in range(8):
                g, d = q // 2, q % 2
                dve.wait_ge(h0_ready, q + 1)
                dec = per_head(EX[:, EXD + 32 * d + g * HPG:EXD + 32 * d + (g + 1) * HPG])
                if q >= 2:
                    dve.wait_ge(yoff_done, 2 * (q - 2) + 2)
                vec.tensor_tensor(heads(H1[:, q % 2, :]), heads(H0[:, q % 2, :]), dec, ALU.mult).then_inc(h_decayed, 1)
                dve.wait_ge(h_decayed, q + 1)
                dve.wait_ge(states, 2 * q + 2)
                vec.tensor_tensor(H1[:, q % 2, :], H1[:, q % 2, :], bank[1][:, :], ALU.add).then_inc(h1_ready, 1)
                if q == 0:
                    dve.wait_ge(cbm_ready, 4)
                for m in range(4 * q, 4 * q + 4):
                    c2, half = chunk_of(m)
                    dve.wait_ge(e_ready, m + 1)
                    if m >= 4:
                        dve.wait_ge(ydiag_done, m - 3)
                    cb = CBm[:, d, c2, g, :].rearrange("p (a n) -> p a n", a=1).broadcast_to([P, 4, P])
                    vec.tensor_tensor(Mb[:, m % 4], Eb[:, m % 2], cb, ALU.mult).then_inc(m_ready, 1)
                    if q < 7:
                        prep_dm(m + 4)
                if q < 7:
                    prep_x(q + 1)
                for o in range(2):
                    c2 = o ^ d
                    dve.wait_ge(yoff_done, 2 * q + o + 1)
                    e = per_head(EX[:, EXC + 64 * c2 + 32 * d + g * HPG:EXC + 64 * c2 + 32 * d + (g + 1) * HPG])
                    vec.tensor_tensor(heads(scr[:, 2 * d + c2, :]), heads(bank[4 + o][:, :]), e, ALU.mult)\
                        .then_inc(toff_ready, 1)
                if d == 1:
                    dve.wait_ge(toff_ready, 2 * q + 2)
                    for c2 in range(2):
                        n = 4 * (2 * g + c2)
                        vec.tensor_tensor(sqb[:, 0, :], scr[:, c2, :], scr[:, 2 + c2, :], ALU.add).then_inc(y_part, 1)
                        dd = per_head(pv[:, PV_D + g * HPG:PV_D + (g + 1) * HPG])
                        vec.tensor_tensor(heads(sqb[:, 1, :]), x_of(2 + c2, g), dd, ALU.mult).then_inc(y_part, 1)
                        dve.wait_ge(y_part, n + 2)
                        vec.tensor_tensor(sqacc[:, :], sqb[:, 0, :], sqb[:, 1, :], ALU.add).then_inc(y_part, 1)
                        dve.wait_ge(y_part, n + 3)
                        dve.wait_ge(ydiag_done, 4 * q + 4)
                        vec.tensor_tensor(tok[:, c2, GW + g * GW:GW + (g + 1) * GW], sqacc[:, :], bank[6 + c2][:, :],
                                          ALU.add).then_inc(y_part, 1)
                    dve.wait_ge(y_part, 8 * g + 8)
            for j in range(8):
                dve.wait_ge(y_turned, j + 1)
                dve.wait_ge(z_ready, 2 * j + 2)
                zz = zT[:, 2 * j:2 * j + 2, :].rearrange("p a n -> p (a n)")
                vec.tensor_tensor(zz, bank[j % 2][:, :], zz, ALU.mult).then_inc(gated, 1)
            for g in range(GROUPS):
                dve.wait_ge(y_std, g + 1)
                vec.reciprocal(sqb[:, g % 2, LAT], sqb[:, g % 2, CTX]).then_inc(y_rst, 1)
                dve.wait_ge(y_rst, g + 1)
                for k in range(4 * g, 4 * g + 4):
                    last = vec.scalar_tensor_tensor(out=zT[:, k, :], in0=zT[:, k, :],
                                                    scalar=pv[:, PV_YG + k:PV_YG + k + 1], in1=sqb[:, g % 2, LAT],
                                                    op0=ALU.mult, op1=ALU.mult)
                last.then_inc(y_full, 1)
                dve.wait_ge(y_hi, g + 1)
                vec.tensor_tensor(ylo[:, 4 * g:4 * g + 4, :], zT[:, 4 * g:4 * g + 4, :],
                                  yhi[:, 4 * g:4 * g + 4, :].bitcast(F32), ALU.subtract).then_inc(y_lo, 1)
            clear_sum(3)
            for t in range(KT):
                lo(C_OUT1 + 2 * t + 2)
                lo(C_OUT1 + 2 * t + 3)
                dve.wait_ge(chunk_used, C_OUT1 + 2 * t + 2)
                residual(8, t, t % 2, (LAT,), lambda h: slice(0, NLAT))
                add_square(3, t, cols=LAT)
            norm(3, (LAT,))
            with dve.Fori(0, 5) as i:
                for p in range(4):
                    ffn_in(1, p, 4, i)
            for p in range(20, FT):
                ffn_in(1, p)
            for t in range(KT):
                for k in range(4):
                    lo(C_FO1 + 4 * t + k + 2)
                dve.wait_ge(chunk_used, C_FO1 + 4 * t + 4)
                residual(11, t, t % 2, (LAT,), lambda h: slice(0, NLAT))

        @block.tensor
        def _(pe):
            mm = nc.tensor.matmul

            def turn(dst, src):
                return nc.tensor.transpose(dst, src, ident)

            def chunk(dst, c, xhi, xlo, k0_, n, first, last, per=0, i=None, ready=None):
                pe.wait_ge(lo_ready, at(c + 1, per, i))
                s = c % RING
                for j in range(n):
                    if ready is not None:
                        pe.wait_ge(ready[0], ready[1] + k0_ + j + 1)
                    for w, xx, o in ((whi, xhi, 0), (whi, xlo, 1), (wlo, xhi, 2)):
                        ins = mm(dst, w[:, s, j * P:(j + 1) * P], xx[:, k0_ + j],
                                 start=first and j == 0 and o == 0, stop=last and j == n - 1 and o == 2)
                ins.then_inc(chunk_used, 1)

            def norm(k, cols):
                pe.wait_ge(sq_added, 9 * k + 9)
                mm(bank[7][:, cols], ones, sqacc[:, cols], start=True, stop=True).then_inc(norm_sum, 1)

            def ada_total(u, per=0, i=None):
                pe.wait_ge(ada_used, at(KT * (u + 1), KT * per, i))
                if u or i is not None:
                    pe.wait_ge(mods_ready, at(u + 2, per, i))
                for t in range(KT):
                    for c in range(2):
                        ins = mm(bank[4][:, 2 * t + c:2 * t + c + 1], aacc[:, c, t * P:(t + 1) * P], ones[:, 0:1],
                                 start=True, stop=True)
                ins.then_inc(ada_sum, 1)

            def ffn_in(l, p, per=0, i=None):
                cbase, fbase = (C_FI0, C_FI1)[l], (F_FI0, F_FI1)[l]
                cols = (ALL, LAT)[l]
                pe.wait_ge(freed, at(fbase + p - 1, per, i))
                for k in range(2):
                    ready = (hlo_ready, KT * (1 + 2 * l)) if p == 0 and k == 0 else None
                    chunk(bank[2 * (p % 2) + k][:, cols], cbase + 2 * p + k, hhi[:, :, cols], hlo[:, :, cols], 0, KT,
                          True, True, 2 * per, i, ready)

            def ffn_out(l, t):
                cbase, fbase = (C_FO0, C_FO1)[l], (F_FO0, F_FO1)[l]
                cols, dst = (ALL, LAT)[l], (ALL, slice(0, NLAT))[l]
                if t >= 2:
                    pe.wait_ge(freed, fbase + t - 1)
                else:
                    pe.wait_ge(freed, fbase)
                for k in range(4):
                    ready = (alo_ready, FT * l) if t == 0 else None
                    chunk(bank[t % 2][:, dst], cbase + 4 * t + k, ahi[:, :, cols], alo[:, :, cols], FO_AT[k],
                          FO_KT[k], k == 0, k == 3, ready=ready)

            pe.wait_ge(const_in, 48)
            pe.wait_ge(cond_silu, 1)
            for n in range(4):
                pe.wait_ge(ada0_in[n], 16)
                for f in range(4):
                    col = 32 + 16 * (n // 2) + 2 * (4 * (n % 2) + f)
                    for k in range(KT):
                        ins = mm(bank[4][:, col:col + 2], ada0[:, n, k, f * P:(f + 1) * P], silc[:, 2 * k:2 * k + 2],
                                 start=k == 0, stop=k == KT - 1)
                if n % 2:
                    ins.then_inc(ada0_sum, 1)
                if n == 0:
                    norm(0, ALL)

            n_sum = n_rot = 0
            srcs = {"gv": gvT, "k": kT, "q": qT}
            for s in range(STEPS0):
                if s < N_IN0:
                    if s >= 4:
                        pe.wait_ge(in0_out, s - 3)
                    chunk(bank[s % 4][:, :], s, hhi, hlo, 0, KT, True, True,
                          ready=(hlo_ready, 0) if s == 0 else None)
                if s in (4, 8):
                    ada_total(s // 4 - 1)
                for name, j in ITEMS.get(s - 1, []):
                    n = n_sum
                    pe.wait_ge(it_sq, n + 1)
                    if n >= 2:
                        pe.wait_ge(it_std, n - 1)
                    w = ones if name == "gv" else k0[:, A_BLK:A_BLK + P]
                    mm(bank[5 + n % 2][:, :], w, isq[:, n % 2, :], start=True, stop=True).then_inc(it_sum, 1)
                    n_sum += 1
                for name, j in ITEMS.get(s - 2, []):
                    if name == "gv":
                        continue
                    pe.wait_ge(it_scaled, ORDER.index((name, j)) + 1)
                    if n_rot:
                        pe.wait_ge(roped, n_rot)
                    mm(bank[7][:, 0:NLAT], k0[:, A_ROT:A_ROT + P], srcs[name][:, j, LAT], start=True, stop=True)\
                        .then_inc(rot_done, 1)
                    n_rot += 1
            for j in range(5):
                pe.wait_ge(in0_out, N_IN0)
                if j >= 2:
                    pe.wait_ge(toks_ready, j - 1)
                if j:
                    pe.wait_ge(it_scaled, ORDER.index(("gv", j - 1)) + 1)
                for tt in range(4):
                    src = vT[:, tt * P:(tt + 1) * P] if j == 0 else gvT[:, j - 1, tt * P:(tt + 1) * P]
                    ins = turn(bank[2 + j % 2][:, tt * P:(tt + 1) * P], src)
                ins.then_inc(turned, 1)
            for n in range(37):
                if n < 32:
                    qb, kv, i = UNITS[n]
                    keys, rows = P * key_tiles(qb), slice(kv * HD, (kv + 1) * HD)
                    if n == 0:
                        pe.wait_ge(roped, len(ROPED))
                        pe.wait_ge(toks_ready, 5)
                    if n >= 2:
                        pe.wait_ge(exp_done, n - 1)
                    mm(bank[n % 2][:, 0:keys], qT[rows, i, qb * P:(qb + 1) * P], kT[rows, 0, 0:keys],
                       start=True, stop=True).then_inc(scores_ready, 1)
                m = n - 2
                if 0 <= m < 32:
                    pe.wait_ge(probs_ready, m + 1)
                    if m >= 2:
                        pe.wait_ge(probT_ready, m - 1)
                    for tt in range(key_tiles(UNITS[m][0])):
                        ins = turn(bank[2 + m % 2][:, tt * P:(tt + 1) * P], prob[:, m % 3, tt * P:(tt + 1) * P])
                    ins.then_inc(probs_turned, 1)
                if n >= 7 and n % 4 == 3:
                    grp = n // 4 - 1
                    qb, kv, _ = UNITS[4 * grp]
                    rows, kts = slice(kv * HD, (kv + 1) * HD), key_tiles(qb)
                    pe.wait_ge(probT_ready, 4 * grp + 4)
                    if qb >= 2:
                        pe.wait_ge(att_lo, qb - 1)
                    for tt in range(kts):
                        ins = mm(bank[5 + qb % 2][rows, :], toks[:, 0, tt, kv * HD:(kv + 1) * HD],
                                 probT[:, grp % 2, tt, :, :].rearrange("p a n -> p (a n)"),
                                 start=tt == 0, stop=tt == kts - 1)
                    ins.then_inc(pv_done, 1)
                if n % 8 == 6 and n < 32:
                    g = n // 8
                    pe.wait_ge(mods_ready, 4)
                    if g:
                        pe.wait_ge(sgu_biased, g)
                    for tt in range(4):
                        w = k0[:, A_SGW + g * P:A_SGW + (g + 1) * P]
                        ins = mm(bank[4][:, tt * P:(tt + 1) * P], toks[:, 1 + g, tt, :], w, start=True, stop=True)
                    ins.then_inc(spatial, 1)
            for t in range(KT):
                if t >= 2:
                    pe.wait_ge(freed, F_OUT0 + t - 1)
                if t == 0:
                    pe.wait_ge(att_lo, 4)
                    pe.wait_ge(sgu_lo, 4)
                chunk(bank[t % 2][:, :], C_OUT0 + t, hhi, hlo, 0, KT, True, True)
            ada_total(2)
            norm(1, ALL)
            with pe.Fori(0, 5) as i:
                for p in range(4):
                    ffn_in(0, p, 4, i)
                ada_total(U_FI0, 1, i)
            for p in range(20, FT):
                ffn_in(0, p)
            for t in range(KT):
                ffn_out(0, t)
                if t in (1, 3):
                    ada_total(U_FO0 + t // 2)
            norm(2, ALL)

            def project(j, cols, per=0, i=None):
                if 4 <= j < 29:
                    pe.wait_ge(freed, at(F_IN1 + j - 3, per, i))
                elif j >= 29:
                    pe.wait_ge(z_ready, j - 28)
                n = cols.stop - cols.start
                chunk(bank[j % 4][:, 0:n], C_IN1 + j, hhi[:, :, cols], hlo[:, :, cols], 0, KT, True, True, per, i,
                      (hlo_ready, 2 * KT) if j == 0 else None)

            def turn_conv(e, per=0, i=None):
                pe.wait_ge(conv_silu, at(e + 1, per, i))
                if e >= 2:
                    pe.wait_ge(tok_ready, at(e - 1, per, i))
                for tt in range(4):
                    ins = turn(bank[4 + e % 2][:, tt * P:(tt + 1) * P], scr[:, 2 + e % 2, tt * P:(tt + 1) * P])
                ins.then_inc(conv_turned, 1)

            project(0, ALL)
            project(1, ALL)
            turn_conv(0)
            project(2, ALL)
            project(3, ALL)
            turn_conv(1)
            pe.wait_ge(freed, F_IN1 + 3)
            for tt in range(4):
                ins = turn(bank[6][:, tt * P:(tt + 1) * P], sqb[:, 0, tt * P:(tt + 1) * P])
            ins.then_inc(dt_turned, 1)
            project(4, ALL)
            turn_conv(2)
            pe.wait_ge(dt_chain, 17)
            for c2 in range(2):
                for d in range(2):
                    col = EXC + 64 * c2 + 32 * d
                    mm(bank[7][:, col:col + 32], incl[d], da[:, 2 + c2, 32 * d:32 * d + 32], start=True, stop=True)
            for n, (d, tt) in enumerate(SPANS):
                rest = {(0, 0): 1, (1, 1): 0}.get((d, tt))
                col = EXW + 32 * n
                mm(bank[7][:, col:col + 32], strict[d], da[:, tt, 32 * d:32 * d + 32], start=True, stop=rest is None)
                if rest is not None:
                    mm(bank[7][:, col:col + 32], ones, da[:, rest, 32 * d:32 * d + 32], start=False, stop=True)
            for d in range(2):
                col = EXD + 32 * d
                ins = mm(bank[7][:, col:col + 32], ones, da[:, 2 + d, 32 * d:32 * d + 32], start=True, stop=True)
            ins.then_inc(sums_done, 1)
            with pe.Fori(0, 4) as i:
                for k in range(4):
                    project(5 + k, ALL, 4, i)
                    turn_conv(3 + k, 4, i)
            for k in range(GROUPS):
                project(21 + k, LAT)
                if k == 0:
                    turn_conv(19)
            for k in range(ZT):
                project(25 + k, LAT)
                if k == 0:
                    pe.wait_ge(conv_silu, 24)
                    pe.wait_ge(bt_ready, GROUPS)
                    pe.wait_ge(tok_ready, 20)
                    for c2 in range(2):
                        for g in range(GROUPS):
                            ins = mm(bank[5 + c2][:, g * P:(g + 1) * P], BT[:, g, c2 * P:(c2 + 1) * P],
                                     CT[:, g, c2 * P:(c2 + 1) * P], start=True, stop=True)
                        ins.then_inc(cb_done, 1)

            pe.wait_ge(z_ready, ZT)
            pe.wait_ge(cbm_ready, 4)

            def seg(m):
                pe.wait_ge(dm_ready, m + 1)
                if m >= 2:
                    pe.wait_ge(e_ready, m - 1)
                mm(bank[2 + m % 2][:, :], strict[(m // 4) % 2], DM[:, m % 4].rearrange("p a n -> p (a n)"),
                   start=True, stop=True).then_inc(seg_done, 1)

            def ydiag(m):
                q, i = m // 4, m % 4
                c2, half = (i // 2) ^ (q % 2), i % 2
                pe.wait_ge(m_ready, m + 1)
                if q >= 2 and q % 2 == 0:
                    pe.wait_ge(y_part, 4 * q)
                for hh in range(4):
                    col = (4 * half + hh) * HD
                    ins = mm(bank[6 + c2][:, col:col + HD], Mb[:, m % 4, hh, :], xs_[:, q % 2, 3 + c2, col:col + HD],
                             start=q % 2 == 0 and half == 0 and hh == 0, stop=q % 2 == 1 and half == 1 and hh == 3,
                             skip_group_check=True)
                ins.then_inc(ydiag_done, 1)

            for q in range(8):
                g, d = q // 2, q % 2
                b_tok = tok[:, :, g * P:(g + 1) * P]
                if q:
                    pe.wait_ge(h0_ready, q)
                    pe.wait_ge(h1_ready, q)
                pe.wait_ge(x_ready, 5 * q + 2)
                for tt in range(2):
                    ins = mm(bank[0][:, :], b_tok[:, tt, :], xs_[:, q % 2, tt, :], start=tt == 0, stop=tt == 1)
                ins.then_inc(states, 1)
                pe.wait_ge(x_ready, 5 * q + 5)
                mm(bank[1][:, :], b_tok[:, 2 + d, :], xs_[:, q % 2, 2, :], start=True, stop=True).then_inc(states, 1)
                seg(4 * q)
                seg(4 * q + 1)
                for o in range(2):
                    c2 = o ^ d
                    if o == 0:
                        pe.wait_ge(h0_ready, q + 1)
                    else:
                        seg(4 * q + 2)
                        ydiag(4 * q)
                        seg(4 * q + 3)
                        ydiag(4 * q + 1)
                        pe.wait_ge(h1_ready, q + 1)
                    if q:
                        pe.wait_ge(toff_ready, 2 * (q - 1) + o + 1)
                    mm(bank[4 + o][:, :], CT[:, g, c2 * P:(c2 + 1) * P], (H0, H1)[o][:, q % 2, :], start=True,
                       stop=True).then_inc(yoff_done, 1)
                ydiag(4 * q + 2)
                ydiag(4 * q + 3)
            pe.wait_ge(y_part, 32)

            def y_total(g):
                if g >= 2:
                    pe.wait_ge(y_std, g - 1)
                for k in range(4):
                    j = 2 * g + k // 2
                    pe.wait_ge(y_sq, j + 1)
                    ins = mm(bank[2 + g % 2][:, 0:NLAT], ones, scr[:, j % 4, (k % 2) * NLAT:(k % 2 + 1) * NLAT],
                             start=k == 0, stop=k == 3)
                ins.then_inc(y_sum, 1)

            for j in range(8):
                if j >= 2:
                    pe.wait_ge(gated, j - 1)
                for k in range(2):
                    for c2 in range(2):
                        f = GW + (2 * j + k) * P
                        ins = turn(bank[j % 2][:, k * NLAT + c2 * P:k * NLAT + (c2 + 1) * P], tok[:, c2, f:f + P])
                ins.then_inc(y_turned, 1)
                if j >= 3 and j % 2:
                    y_total(j // 2 - 1)
            y_total(3)
            for t in range(KT):
                if t >= 2:
                    pe.wait_ge(freed, F_OUT1 + t - 1)
                if t == 0:
                    pe.wait_ge(y_lo, GROUPS)
                for k in range(2):
                    chunk(bank[t % 2][:, 0:NLAT], C_OUT1 + 2 * t + k, yhi, ylo, KT * k, KT, k == 0, k == 1)
            norm(3, LAT)
            with pe.Fori(0, 5) as i:
                for p in range(4):
                    ffn_in(1, p, 4, i)
            for p in range(20, FT):
                ffn_in(1, p)
            for t in range(KT):
                ffn_out(1, t)


def tiles(w, k_per=KT):
    k, n = w.shape
    w = w.reshape(k // P, P, n // P, P).transpose(2, 1, 0, 3).reshape(n // P, P, k // P, P)
    w = w.reshape(n // P, P, k // P // k_per, k_per * P).transpose(0, 2, 1, 3)
    return np.ascontiguousarray(w.reshape(-1, P, k_per * P))


def columns(v):
    return v.reshape(-1, P).T


def constants():
    f = np.float32
    t = np.arange(P)
    k = np.concatenate([np.eye(P), np.ones((P, P)), t[:, None] <= t, t[:, None] >= t, t[:, None] > t,
                        t[:, None] < t], axis=1).astype(f)
    tt = np.arange(NLAT)
    inv = f(10000.0) ** (-np.arange(HD // 4, dtype=f) / f(HD // 4))
    ang = np.concatenate([(tt // 64).astype(f)[:, None] * inv, (tt % 64).astype(f)[:, None] * inv], axis=1)
    cos, sin = (np.tile(fn(ang).astype(f).T, (4, 1)) for fn in (np.cos, np.sin))
    rot = np.zeros((P, P), f)
    for j in range(P):
        if j % HD < HD // 2:
            rot[j + HD // 2, j] = -1
        else:
            rot[j - HD // 2, j] = 1
    blk = (t[:, None] // HD == t // HD).astype(f)
    return k, np.concatenate([cos, sin, rot, blk], axis=1)


def kernel(**inputs):
    import concourse.bacc as bacc
    from concourse.bass_utils import run_bass_kernel_spmd

    a = {k: np.asarray(v) for k, v in inputs.items()}
    cat = np.concatenate
    k, k0 = constants()
    sgw = a["sgu_w"][0].transpose(2, 0, 1).reshape(P, GROUPS * P)
    k0 = cat([k0, sgw, np.tile(a["sgu_b"].reshape(1, -1), (P, 1))], axis=1)
    perm = cat([np.arange(h * HD, (h + 1) * HD) for i in range(4) for h in (i, i + 4)])
    w = a["mix_w_in"][0]
    w_in0 = tiles(cat([w[:, 1280:1792], w[:, 768:1280], w[:, 512:640], w[:, 640:768], w[:, :512][:, perm]], axis=1))
    w = a["mix_w_out"][0]
    w_out0 = tiles(cat([w[:512][perm], w[512:]], axis=0))
    w_fi = []
    for l in range(2):
        t = tiles(a["ffn_w_in"][l])
        w_fi.append(np.stack([t[:FT], t[FT:]], axis=1).reshape(2 * FT, P, CW))
    w_fi = cat(w_fi)
    w_fo = cat([tiles(a["ffn_w_out"][l], FT) for l in range(2)])
    w = a["ssm_w_in"][0]
    z, x, b, c, dt = (w[:, s] for s in (slice(0, 2048), slice(2048, 4096), slice(4096, 4608), slice(4608, 5120),
                                        slice(5120, 5184)))
    w_in1 = tiles(cat([b[:, :256], dt, dt, b[:, 256:], x, c, z], axis=1))
    w_out1 = tiles(a["ssm_w_out"][0])
    ada_w = np.ascontiguousarray(a["ada_w"].reshape(2, D, 6, D).transpose(0, 2, 1, 3).reshape(12, D, D))
    cond = np.stack([a["c_ctx"].reshape(-1), a["c"].reshape(-1)], axis=1).reshape(KT, P, 2)
    norms = cat([a["norm1_g"][0], a["norm2_g"][0], a["norm1_g"][1], a["norm2_g"][1]])
    order = cat([np.arange(16, 20), np.arange(16), np.arange(20, 24)])
    pvec = cat([cond.transpose(1, 0, 2).reshape(P, 2 * KT), columns(a["ada_b"].reshape(-1)), columns(norms),
                np.tile(a["q_norm_g"][0], 2)[:, None], np.tile(a["k_norm_g"][0], 2)[:, None],
                columns(a["sgu_norm_g"][0]),
                *(columns(a["ssm_conv_w"][0, tap])[:, order] for tap in range(3)),
                columns(a["ssm_conv_b"][0])[:, order],
                np.tile(a["ssm_dt_bias"].reshape(-1), 2)[:, None], columns(a["ssm_norm_g"][0]),
                np.tile(a["ssm_a_log"].reshape(1, -1), (P, 1)), np.tile(a["ssm_d"].reshape(1, -1), (P, 1)),
                np.full((P, 1), EPS, np.float32)], axis=1)
    x_in = cat([a["ctx"][0], a["x"][0]], axis=0).T.reshape(KT, P, T).transpose(1, 0, 2)
    arrays = {"x_in": x_in, "consts": k, "consts0": k0, "pvec": pvec, "ada_w": ada_w, "w_in0": w_in0,
              "w_out0": w_out0, "w_fi": w_fi, "w_fo": w_fo, "w_in1": w_in1, "w_out1": w_out1}
    arrays = {n: np.ascontiguousarray(v) for n, v in arrays.items()}
    nc = bacc.Bacc("TRN2", target_bir_lowering=False, num_devices=1)
    args = [nc.dram_tensor(f"in_{n}", v.shape, mybir.dt.from_np(v.dtype), kind="ExternalInput").ap()
            for n, v in arrays.items()]
    out = nc.dram_tensor("out_x", (KT, P, NLAT), F32, kind="ExternalOutput").ap()
    build(nc, *args, out)
    r = run_bass_kernel_spmd(nc, [{f"in_{n}": v for n, v in arrays.items()}], core_ids=[0])
    got = r.results[0]["out_x"]
    return np.ascontiguousarray(got.transpose(2, 0, 1).reshape(1, NLAT, D))
```

```python
from contextlib import ExitStack

import numpy as np

import concourse.bass as bass
from concourse import mybir

F32 = mybir.dt.float32
F32R = mybir.dt.float32r
ALU = mybir.AluOpType
ACT = mybir.ActivationFunctionType
AX_X = mybir.AxisListType.X

P = 128
D = 1024
KT = D // P
NCTX = 256
NLAT = 256
T = NCTX + NLAT
CTX, LAT, ALL = slice(0, NCTX), slice(NCTX, T), slice(0, T)
HALVES = (CTX, LAT)
FFN = 2816
FT = FFN // P
HD = 64
GROUPS = 4
INNER = 2048
ZT = INNER // P
HPG = 8
GW = HPG * HD
NDT = 64
EPS = 1e-6
CW = KT * P
RING = 4

C_IN0 = 0
N_IN0 = 14
C_OUT0 = C_IN0 + N_IN0
C_FI0 = C_OUT0 + KT
C_FO0 = C_FI0 + 2 * FT
C_IN1 = C_FO0 + 4 * KT
N_IN1 = 41
C_OUT1 = C_IN1 + N_IN1
C_FI1 = C_OUT1 + 2 * KT
C_FO1 = C_FI1 + 2 * FT
C_END = C_FO1 + 4 * KT
C_VEC = C_OUT1 + 2
FO_KT = (6, 6, 5, 5)
FO_AT = (0, 6, 12, 17)

F_OUT0 = 0
F_FI0 = F_OUT0 + KT
F_FO0 = F_FI0 + FT
F_IN1 = F_FO0 + KT
F_OUT1 = F_IN1 + 25
F_FI1 = F_OUT1 + KT
F_FO1 = F_FI1 + FT

N_UNITS = 10
U_FI0 = 4
U_FO0 = 9
U_LAT = 8

K_ID, K_ONE, K_LE, K_GE, K_GT, K_LT = (i * P for i in range(6))
K_W = 6 * P
PV_COND = 0
PV_ADAB = PV_COND + 2 * KT
PV_G = PV_ADAB + 12 * KT
PV_QG = PV_G + 4 * KT
PV_KG = PV_QG + 1
PV_SG = PV_KG + 1
PV_CW = PV_SG + GROUPS
PV_CB = PV_CW + 72
PV_DTB = PV_CB + 24
PV_YG = PV_DTB + 1
PV_AL = PV_YG + ZT
PV_D = PV_AL + NDT
PV_EPS = PV_D + 32
PV_W = PV_EPS + 1
A_COS, A_SIN, A_ROT, A_BLK, A_SGW, A_SGB = 0, 256, 512, 640, 768, 1280
A_W = 1792

ARENA = 2 * FT * T

J_K, J_V, J_Q, J_U = 4, 5, 6, 10
N_DENSE = 11
ITEMS = {3: [("gv", 0)], 4: [("gv", 1), ("k", 0)], 5: [("gv", 2)], 6: [("gv", 3), ("q", 0)],
         7: [("q", 1)], 8: [("q", 2)], 9: [("q", 3)]}
ORDER = [it for s in sorted(ITEMS) for it in ITEMS[s]]
ROPED = [it for it in ORDER if it[0] != "gv"]
STEPS0 = 12
ADA_AT = {0: (0, 1), 1: (2, 3), 2: (4,), 3: (5,), 4: (6,), 5: (7,), 6: (8, 9), 7: (10,), 8: (11, 12), 9: (13,),
          10: (14,)}
ADA_WITH = {3: (0, 1), 4: (2, 3), 5: (4, 5), 6: (6,), 7: (7,), 8: (8,), 9: (9,), 10: (10, 11), 11: (12,),
            12: (13, 14), 13: (15,)}

UNITS = [(qb, kv, i) for qb in range(T // P) for kv in range(2) for i in range(4)]


def key_tiles(qb):
    return 2 if qb < 2 else 4


def at(const, per=0, i=None):
    return const if i is None else const + per * i


def chunk_width(c):
    for base in (C_FO0, C_FO1):
        if base <= c < base + 4 * KT:
            return FO_KT[(c - base) % 4] * P
    return CW


def conv_taps(tile):
    return [PV_CW + tap * 24 + tile for tap in range(3)]


def build(nc, x_in, consts, consts0, pvec, crow, ada_w, ada_t, w_in0, w_out0, w_fi, w_fo, w_in1, w_out1, out):
    with ExitStack() as ctx:
        def sb(name, shape, dt=F32):
            return ctx.enter_context(nc.sbuf_tensor(name, shape, dt))

        def over(name, region, col, shape, dt=F32):
            return nc.alloc_sbuf_tensor_at(name, shape, dt, offset=region + 4 * col)

        def sem(name):
            return ctx.enter_context(nc.semaphore(name))

        kc = sb("kc", [P, K_W])
        pv = sb("pv", [P, PV_W])
        xT = sb("xT", [P, KT, T])
        whi = sb("whi", [P, RING, CW], F32R)
        silc = sb("silc", [P, 2 * KT])
        mod = sb("mod", [P, 12, KT, 2])
        gain = sb("gain", [P, 4, KT, 2])
        attn_s = sb("attn_s", [P, 4, 4])
        warm = sb("warm", [P, 1])
        asum = sb("asum", [P, KT, 2])
        junk = sb("junk", [P, D])
        ystd = sb("ystd", [P, 2 * GROUPS])
        yrst = sb("yrst", [P, 2 * GROUPS])
        nstd = sb("nstd", [P, 4])
        nrst = sb("nrst", [P, 4])
        base = (nc.sbuf_base + 31) // 32 * 32
        r_raw = base
        r_h = r_raw + 4 * RING * CW
        r_ada = r_h + 4 * 2 * KT * T
        r_scr = r_ada + 4 * 4 * D
        r_arena = r_scr + 4 * 7 * T
        assert r_arena + 4 * ARENA <= nc.sbuf_usable_end, (r_arena + 4 * ARENA, nc.sbuf_usable_end)

        raw = over("raw", r_raw, 0, [P, RING, CW])
        wlo = over("wlo", r_raw, 0, [P, RING, CW], F32R)
        hhi = over("hhi", r_h, 0, [P, KT, T], F32R)
        hlo = over("hlo", r_h, KT * T, [P, KT, T], F32R)
        aring = over("aring", r_ada, 0, [P, 2, D])
        csil = over("csil", r_ada, 2 * D, [P, 2, D])
        scr = over("scr", r_scr, 0, [P, 4, T])
        sqb = over("sqb", r_scr, 4 * T, [P, 2, T])
        sqacc = over("sqacc", r_scr, 6 * T, [P, T])
        ahi = over("ahi", r_arena, 0, [P, FT, T], F32R)
        alo = over("alo", r_arena, FT * T, [P, FT, T], F32R)
        k0 = over("k0", r_arena, ARENA - A_W, [P, A_W])
        ada0 = over("ada0", r_arena, 0, [P, 4, KT, 512])
        rows0 = over("rows0", r_arena, 4 * KT * 512, [P, 4, 512])
        cur = [0]

        def arena(name, shape):
            col = cur[0]
            cur[0] += int(np.prod(shape[1:]))
            assert cur[0] <= ARENA, name
            return over(name, r_arena, col, shape)

        qT = arena("qT", [P, 4, T])
        kT = arena("kT", [P, 1, T])
        vT = arena("vT", [P, T])
        uT = arena("uT", [P, GROUPS, T])
        gvT = arena("gvT", [P, GROUPS, T])
        toks = arena("toks", [P, 5, 4, P])
        prob = arena("prob", [P, 3, T])
        probT = arena("probT", [P, 2, 4, 4, P])
        isq = arena("isq", [P, 2, T])
        istd = arena("istd", [P, 2, 8])
        irst = arena("irst", [P, 2, 8])
        ibc = arena("ibc", [P, 2, T])
        rtmp = arena("rtmp", [P, 2, NLAT])
        assert cur[0] <= ARENA - A_W
        cur[0] = 0
        zT = arena("zT", [P, ZT, NLAT])
        tok = arena("tok", [P, 4, GW + INNER])
        CT = arena("CT", [P, GROUPS, NLAT])
        CBm = arena("CBm", [P, 2, 2, GROUPS, P])
        BT = arena("BT", [P, GROUPS, NLAT])
        dts = arena("dts", [P, 8, 4 * NDT])
        dt_ = arena("dt_", [P, 4, NDT])
        da = arena("da", [P, 4, NDT])
        expa = arena("expa", [P, NDT])
        EX = arena("EX", [P, 384])
        dtW = arena("dtW", [P, 6, 32])
        xs_ = over("xs_", r_h, 0, [P, 2, 5, GW])
        DM = over("DM", r_h, 10 * GW, [P, 4, 4, P])
        Eb = over("Eb", r_h, 14 * GW, [P, 2, 4, P])
        H0 = over("H0", r_ada, 0, [P, 2, GW])
        H1 = over("H1", r_ada, 2 * GW, [P, 2, GW])
        Mb = over("Mb", r_ada, 4 * GW, [P, 4, 4, P])
        yhi = hhi[:, :, :].rearrange("p k (a n) -> p (k a) n", a=2)
        ylo = hlo[:, :, :].rearrange("p k (a n) -> p (k a) n", a=2)
        EXC, EXW, EXD = 0, 128, 320
        SPANS = [(0, 0), (0, 1), (0, 2), (1, 0), (1, 1), (1, 3)]

        bank = [ctx.enter_context(nc.psum_tensor(f"bank{b}", [P, 512], F32)) for b in range(8)]

        ident = kc[:, K_ID:K_ID + P]
        ones = kc[:, K_ONE:K_ONE + P]
        incl = [kc[:, K_LE:K_LE + P], kc[:, K_GE:K_GE + P]]
        strict = [kc[:, K_GT:K_GT + P], kc[:, K_LT:K_LT + P]]
        eps = pv[:, PV_EPS:PV_EPS + 1]

        pv_in = sem("pv_in")
        const_in = sem("const_in")
        k0_in = sem("k0_in")
        ada0_rows = sem("ada0_rows")
        rows_out = sem("rows_out")
        x_landed = sem("x_landed")
        ada0_in = [sem(f"ada0_in{i}") for i in range(4)]
        raw_in = [sem(f"raw_in{i}") for i in range(RING)]
        ada_in = [sem(f"ada_in{i}") for i in range(2)]
        hi_ready = sem("hi_ready")
        lo_ready = sem("lo_ready")
        chunk_used = sem("chunk_used")
        cond_silu = sem("cond_silu")
        ada0_sum = sem("ada0_sum")
        ada_used = sem("ada_used")
        ada_half = sem("ada_half")
        crow_in = sem("crow_in")
        crow_silu = sem("crow_silu")
        mods_ready = sem("mods_ready")
        gains_ready = sem("gains_ready")
        squared = sem("squared")
        sq_added = sem("sq_added")
        norm_sum = sem("norm_sum")
        std_ready = sem("std_ready")
        rstd_ready = sem("rstd_ready")
        norm_bc = sem("norm_bc")
        norm_back = sem("norm_back")
        scaled = sem("scaled")
        hhi_ready = sem("hhi_ready")
        hlo_ready = sem("hlo_ready")
        freed = sem("freed")
        in0_out = sem("in0_out")
        it_sq = sem("it_sq")
        it_sum = sem("it_sum")
        it_std = sem("it_std")
        it_rst = sem("it_rst")
        it_bc = sem("it_bc")
        it_back = sem("it_back")
        it_scaled = sem("it_scaled")
        rot_done = sem("rot_done")
        rope_tmp = sem("rope_tmp")
        roped = sem("roped")
        turned = sem("turned")
        toks_ready = sem("toks_ready")
        scores_ready = sem("scores_ready")
        rowmax = sem("rowmax")
        bias_ready = sem("bias_ready")
        exp_done = sem("exp_done")
        recip_done = sem("recip_done")
        probs_ready = sem("probs_ready")
        probs_turned = sem("probs_turned")
        probT_ready = sem("probT_ready")
        pv_done = sem("pv_done")
        att_hi = sem("att_hi")
        att_lo = sem("att_lo")
        spatial = sem("spatial")
        sgu_biased = sem("sgu_biased")
        sgu_full = sem("sgu_full")
        u_gelu = sem("u_gelu")
        sgu_hi = sem("sgu_hi")
        sgu_lo = sem("sgu_lo")
        silu_ready = sem("silu_ready")
        ahi_ready = sem("ahi_ready")
        alo_ready = sem("alo_ready")
        conv_mid = sem("conv_mid")
        conv_left = sem("conv_left")
        conv_silu = sem("conv_silu")
        conv_turned = sem("conv_turned")
        tok_ready = sem("tok_ready")
        bt_ready = sem("bt_ready")
        dt_biased = sem("dt_biased")
        dt_turned = sem("dt_turned")
        dt_chain = sem("dt_chain")
        dt_exp = sem("dt_exp")
        sums_done = sem("sums_done")
        decays = sem("decays")
        dtw_ready = sem("dtw_ready")
        cb_done = sem("cb_done")
        cbm_ready = sem("cbm_ready")
        z_ready = sem("z_ready")
        x_ready = sem("x_ready")
        dm_ready = sem("dm_ready")
        states = sem("states")
        h0_ready = sem("h0_ready")
        h_decayed = sem("h_decayed")
        h1_ready = sem("h1_ready")
        seg_done = sem("seg_done")
        e_ready = sem("e_ready")
        m_ready = sem("m_ready")
        yoff_done = sem("yoff_done")
        toff_ready = sem("toff_ready")
        ydiag_done = sem("ydiag_done")
        y_part = sem("y_part")
        y_ready = sem("y_ready")
        y_turned = sem("y_turned")
        gated = sem("gated")
        y_sq = sem("y_sq")
        y_sum = sem("y_sum")
        y_std = sem("y_std")
        y_rst = sem("y_rst")
        y_bc = sem("y_bc")
        y_back = sem("y_back")
        y_full = sem("y_full")
        y_hi = sem("y_hi")
        y_lo = sem("y_lo")
        stored = sem("stored")

        def per_head(v, n=HD):
            return v.rearrange("p (a n) -> p a n", n=1).broadcast_to([P, v.shape[1], n])

        def heads(v):
            return v.rearrange("p (a n) -> p a n", n=HD)

        def x_of(tt, g):
            return heads(tok[:, tt, GW + g * GW:GW + (g + 1) * GW])

        def chunk_of(m):
            q, i = m // 4, m % 4
            return (i // 2) ^ (q % 2), i % 2

        block = ctx.enter_context(nc.Block())

        @block.sync
        def _(sp):
            sp.dma_start(pv[:, :], pvec).then_inc(pv_in, 16)
            for n in range(4):
                src = ada_w[1 - n // 2, :, (n % 2) * 512:(n % 2 + 1) * 512].rearrange("(k p) n -> p k n", p=P)
                sp.dma_start(ada0[:, n], src).then_inc(ada0_in[n], 16)
                if n == 0:
                    sp.dma_start(kc[:, :], consts).then_inc(const_in, 16)
                if n == 1:
                    sp.dma_start(xT[:, :, :], x_in).then_inc(x_landed, 16)

            def pick(w, n, per=0, i=None):
                return w[bass.ds(at(n, per, i), 1)].rearrange("a p n -> p (a n)")

            def load(src, c, per=0, i=None):
                if c >= RING:
                    sp.wait_ge(chunk_used, at(c - RING + 1, per, i))
                w = chunk_width(c)
                sp.dma_start(raw[:, c % RING, 0:w], src).then_inc(raw_in[c % RING], 16)

            def load_ada(a, per=0, i=None):
                if a >= 2:
                    sp.wait_ge(ada_used, at(a - 1, per, i))
                sp.dma_start(aring[:, a % 2, :], pick(ada_t, a, per, i)).then_inc(ada_in[a % 2], 16)

            sp.dma_start(csil[:, :, :], crow).then_inc(crow_in, 16)
            for c in range(N_IN0):
                load(w_in0[c], C_IN0 + c)
                if c == RING - 1:
                    sp.dma_start(k0[:, :], consts0).then_inc(k0_in, 16)
                for a in ADA_WITH.get(c, ()):
                    load_ada(a)
            for t, units in enumerate(((16, 17), (18, 19, 20), (21, 22), range(23, 28))):
                load(w_out0[t], C_OUT0 + t)
                for a in units:
                    load_ada(a)
            for t in range(4, KT):
                load(w_out0[t], C_OUT0 + t)
                load_ada(24 + t)
            for k in range(8):
                load(w_fi[k], C_FI0 + k)
                if k < 2:
                    load_ada(32 + k)
            with sp.Fori(0, 4) as i:
                for k in range(8):
                    load(pick(w_fi, 8 + k, 8, i), C_FI0 + 8 + k, 8, i)
                    load_ada(C_FI0 + 12 + k, 8, i)
            for k in range(40, 44):
                load(w_fi[k], C_FI0 + k)
                load_ada(C_FI0 + k + 4)
            for t in range(KT):
                for k in range(4):
                    c = C_FO0 + 4 * t + k
                    load(w_fo[t, :, FO_AT[k] * P:(FO_AT[k] + FO_KT[k]) * P], c)
                    if c + 4 < 8 * N_UNITS:
                        load_ada(c + 4)
            for k in range(5):
                load(w_in1[k], C_IN1 + k)
            with sp.Fori(0, 9) as i:
                for k in range(4):
                    load(pick(w_in1, 5 + k, 4, i), C_IN1 + 5 + k, 4, i)
            with sp.Fori(0, 4) as i:
                for k in range(4):
                    load(pick(w_out1, k, 4, i), C_OUT1 + k, 4, i)
            with sp.Fori(0, 11) as i:
                for k in range(4):
                    load(pick(w_fi, 2 * FT + k, 4, i), C_FI1 + k, 4, i)
            for t in range(KT):
                for k in range(4):
                    load(w_fo[KT + t, :, FO_AT[k] * P:(FO_AT[k] + FO_KT[k]) * P], C_FO1 + 4 * t + k)
            for t in range(KT):
                sp.wait_ge(freed, F_FO1 + t + 1)
                sp.dma_start(out[t], xT[:, t, LAT]).then_inc(stored, 16)
            sp.wait_ge(stored, 16 * KT)

        @block.scalar
        def _(act):
            def hi(c, per=0, i=None):
                if c >= C_END:
                    return
                act.wait_ge(raw_in[c % RING], at(16 * (c // RING + 1), 16 * per // RING, i))
                if c >= RING:
                    act.wait_ge(chunk_used, at(c - RING + 1, per, i))
                w = chunk_width(c)
                nc.scalar.activation(whi[:, c % RING, 0:w], raw[:, c % RING, 0:w], ACT.Copy).then_inc(hi_ready, 1)

            def square(k, t, per=0, i=None, cols=ALL):
                if t >= 2:
                    act.wait_ge(sq_added, at(9 * k + t, per, i))
                src = xT[:, bass.ds(at(t, per, i), 1), cols].rearrange("p a n -> p (a n)")
                nc.scalar.activation(sqb[:, t % 2, cols], src, ACT.Square).then_inc(squared, 1)

            def preload_sqrt():
                nc.scalar.activation(warm[:, 0:1], eps, ACT.Sqrt)

            def norm_std(k, halves):
                tts = slice(halves[0].start // P, 4)
                act.wait_ge(norm_sum, k + 1)
                nc.scalar.activation(nstd[:, tts], bank[7][:, tts], ACT.Sqrt, bias=eps,
                                     scale=1.0 / D).then_inc(std_ready, 1)

            def norm(k, halves):
                shift = 6 * (k // 2) + 3 * (k % 2)
                for t in range(KT):
                    act.wait_ge(scaled, KT * k + t + 1)
                    for h in halves:
                        c = 0 if h is CTX else 1
                        last = nc.scalar.activation(hhi[:, t, h], scr[:, t % 2, h], ACT.Identity,
                                                    bias=mod[:, shift, t, c:c + 1])
                    last.then_inc(hhi_ready, 1)

            def ffn_in(l, p, per=0, i=None):
                cbase, fbase = (C_FI0, C_FI1)[l], (F_FI0, F_FI1)[l]
                cols = (ALL, LAT)[l]
                pi = None if i is None else i
                hi(cbase + 2 * p + 2, 2 * per, pi)
                hi(cbase + 2 * p + 3, 2 * per, pi)
                act.wait_ge(chunk_used, at(cbase + 2 * p + 1, 2 * per, pi))
                act.wait_ge(freed, at(fbase + p - 1, per, pi))
                nc.scalar.activation(scr[:, p % 2, cols], bank[2 * (p % 2)][:, cols], ACT.Silu).then_inc(silu_ready, 1)
                act.wait_ge(freed, at(fbase + p + 1, per, pi))
                dst = ahi[:, bass.ds(at(p, per, pi), 1), cols].rearrange("p a n -> p (a n)")
                nc.scalar.activation(dst, scr[:, 2 + p % 2, cols], ACT.Copy).then_inc(ahi_ready, 1)

            act.wait_ge(pv_in, 16)
            nc.scalar.activation(silc[:, :], pv[:, PV_COND:PV_COND + 2 * KT], ACT.Silu).then_inc(cond_silu, 1)
            act.wait_ge(x_landed, 16)
            for t in range(KT):
                square(0, t)
            for n in range(4):
                act.wait_ge(ada0_rows, n + 1)
                nc.scalar.activation(rows0[0:2, n, :], bank[n][0:2, :], ACT.Copy).then_inc(rows_out, 1)
                if n == 2:
                    norm_std(0, HALVES)
                    act.wait_ge(crow_in, 16)
                    nc.scalar.activation(csil[:, :, :], csil[:, :, :], ACT.Silu).then_inc(crow_silu, 1)
                    hi(0)
                    hi(1)
            norm(0, HALVES)

            n_sq = n_std = 0
            srcs = {"gv": gvT, "k": kT, "q": qT}
            def copy_out(c, b):
                act.wait_ge(chunk_used, C_IN0 + c + 1)
                dst = (gvT[:, c, :] if c < J_K else kT[:, 0, :] if c == J_K else vT[:, :] if c == J_V else
                       qT[:, c - J_Q, :] if c < J_U else uT[:, c - J_U, :])
                f = ACT.Gelu_apprx_tanh if c < J_K else ACT.Copy
                nc.scalar.activation(dst, bank[b][:, :], f).then_inc(in0_out, 1)

            for s in range(STEPS0):
                if s < N_DENSE:
                    hi(s + 2)
                for name, j in ITEMS.get(s - 1, []):
                    act.wait_ge(it_sum, n_std + 1)
                    if n_std >= 2:
                        act.wait_ge(it_rst, n_std - 1)
                    w = 4 if name == "gv" else 8
                    nc.scalar.activation(istd[:, n_std % 2, 0:w], bank[5 + n_std % 2][:, 0:w], ACT.Sqrt, bias=eps,
                                         scale=1.0 / (P if name == "gv" else HD)).then_inc(it_std, 1)
                    n_std += 1
                if s < N_DENSE:
                    copy_out(s, s % 4)
                for name, j in ITEMS.get(s, []):
                    if n_sq >= 2:
                        act.wait_ge(it_sum, n_sq - 1)
                    act.wait_ge(in0_out, {"gv": j, "k": J_K, "q": J_Q + j}[name] + 1)
                    nc.scalar.activation(isq[:, n_sq % 2, :], srcs[name][:, j, :], ACT.Square).then_inc(it_sq, 1)
                    n_sq += 1
            for j in range(5):
                act.wait_ge(turned, j + 1)
                nc.scalar.activation(toks[:, j, :, :].rearrange("p a n -> p (a n)"), bank[3 - j % 2][:, :],
                                     ACT.Copy).then_inc(toks_ready, 1)
            for n in range(39):
                if n < 32:
                    keys = P * key_tiles(UNITS[n][0])
                    act.wait_ge(bias_ready, n + 1)
                    if n >= 3:
                        act.wait_ge(probs_turned, n - 2)
                    nc.scalar.activation(prob[:, n % 3, 0:keys], bank[n % 2][:, 0:keys], ACT.Exp,
                                         bias=attn_s[:, n % 4, 1:2], scale=HD ** -0.5,
                                         accum_out=attn_s[:, n % 4, 2:3]).then_inc(exp_done, 1)
                m = n - 2
                if 0 <= m < 32:
                    grp, i, kt = m // 4, m % 4, key_tiles(UNITS[m][0])
                    act.wait_ge(probs_turned, m + 1)
                    if grp >= 2:
                        act.wait_ge(pv_done, grp - 1)
                    nc.scalar.activation(probT[:, grp % 2, 0:kt, i, :],
                                         bank[2 + m % 2][:, 0:kt * P].rearrange("p (a n) -> p a n", n=P),
                                         ACT.Copy).then_inc(probT_ready, 1)
                if n % 4 == 0 and n < 16:
                    if n < 12:
                        hi(N_DENSE + n // 4 + 2)
                    if n:
                        copy_out(N_DENSE + n // 4 - 1, (7, 6, 7)[n // 4 - 1])
                if n % 8 == 4 and n >= 12:
                    qb = (n - 12) // 8
                    act.wait_ge(pv_done, 2 * qb + 2)
                    nc.scalar.activation(hhi[:, 0:4, qb * P:(qb + 1) * P],
                                         bank[5 + qb % 2][:, :].rearrange("p (a n) -> p a n", n=P),
                                         ACT.Copy).then_inc(att_hi, 1)
                if n >= 32:
                    g = n - 32
                    if g < GROUPS:
                        nc.scalar.activation(uT[:, g, :], uT[:, g, :], ACT.Gelu_apprx_tanh).then_inc(u_gelu, 1)
                    if g >= 1 and g - 1 < GROUPS:
                        act.wait_ge(sgu_full, g)
                        nc.scalar.activation(hhi[:, 3 + g, :], uT[:, g - 1, :], ACT.Copy).then_inc(sgu_hi, 1)
            preload_sqrt()
            hi(C_OUT0 + 2)
            for t in range(KT):
                if t < KT - 1:
                    hi(C_OUT0 + t + 3)
                act.wait_ge(freed, F_OUT0 + t + 1)
                square(1, t)
            norm_std(1, HALVES)
            norm(1, HALVES)
            for p in range(2):
                ffn_in(0, p)
            with act.Fori(0, 4) as i:
                for p in range(2, 6):
                    ffn_in(0, p, 4, i)
            for p in range(18, FT):
                ffn_in(0, p)
            preload_sqrt()
            for t in range(KT):
                for k in range(4):
                    hi(C_FO0 + 4 * t + k + 2)
                act.wait_ge(freed, F_FO0 + t + 1)
                square(2, t)
            norm_std(2, HALVES)
            norm(2, HALVES)

            def conv(j, e, per=0, i=None):
                hi(C_IN1 + j + 2, per, i)
                act.wait_ge(chunk_used, at(C_IN1 + j + 1, per, i))
                tap = conv_taps(e)[1]
                cols = slice(0, T) if e < 20 else slice(0, NLAT)
                nc.scalar.activation(scr[:, e % 2, cols], bank[j % 4][:, cols], ACT.Identity,
                                     bias=pv[:, bass.ds(at(PV_CB + e, per, i), 1)],
                                     scale=pv[:, bass.ds(at(tap, per, i), 1)]).then_inc(conv_mid, 1)
                act.wait_ge(freed, at(F_IN1 + j + 1, per, i))
                if e >= 2 and e < 20:
                    act.wait_ge(conv_turned, at(e - 1, per, i))
                    if i is None:
                        act.wait_ge(bt_ready, min(e - 1, GROUPS))
                dst = scr[:, 2 + e % 2, :] if e < 20 else CT[:, e - 20, :]
                nc.scalar.activation(dst, scr[:, e % 2, cols], ACT.Silu).then_inc(conv_silu, 1)

            def tok_out(e, per=0, i=None):
                act.wait_ge(conv_turned, at(e + 1, per, i))
                nc.scalar.activation(tok[:, :, bass.ds(at(e * P, P * per, i), P)],
                                     bank[4 + e % 2][:, :].rearrange("p (a n) -> p a n", n=P),
                                     ACT.Copy).then_inc(tok_ready, 1)

            conv(0, 0)
            conv(1, 1)
            tok_out(0)
            hi(C_IN1 + 2 + 2)
            conv(3, 2)
            tok_out(1)
            conv(4, 3)
            tok_out(2)
            with act.Fori(0, 4) as i:
                for k in range(4):
                    conv(5 + k, 4 + k, 4, i)
                    tok_out(3 + k, 4, i)
            for k in range(GROUPS):
                conv(21 + k, 20 + k)
                if k == 0:
                    tok_out(19)
            for k in range(ZT):
                hi(C_IN1 + 25 + k + 2)
                act.wait_ge(chunk_used, C_IN1 + 25 + k + 1)
                nc.scalar.activation(zT[:, k, :], bank[(25 + k) % 4][:, 0:NLAT], ACT.Silu).then_inc(z_ready, 1)
                if k == 2:
                    act.wait_ge(dt_chain, 1)
                    nc.scalar.activation(dts[:, 1, :], dts[:, 0, :], ACT.Abs).then_inc(dt_exp, 1)
                    act.wait_ge(dt_exp, 1)
                    nc.scalar.activation(dts[:, 2, :], dts[:, 1, :], ACT.Exp, scale=-1.0).then_inc(dt_exp, 1)
                    nc.scalar.activation(expa[:, :], pv[:, PV_AL:PV_AL + NDT], ACT.Exp).then_inc(dt_exp, 1)
                if k == 10:
                    act.wait_ge(sums_done, 1)
                    nc.scalar.activation(EX[:, :], bank[7][:, 0:384], ACT.Exp).then_inc(decays, 1)
            def prep_dm(m):
                q = m // 4
                g, d = q // 2, q % 2
                c2, half = chunk_of(m)
                if m >= 4:
                    act.wait_ge(seg_done, m - 3)
                for hh in range(4):
                    h = 32 * d + g * HPG + 4 * half + hh
                    last = nc.scalar.activation(DM[:, m % 4, hh, :], incl[d], ACT.Copy,
                                                scale=da[:, 2 + c2, h:h + 1])
                last.then_inc(dm_ready, 1)

            def y_square(g):
                for j in (2 * g, 2 * g + 1):
                    act.wait_ge(gated, j + 1)
                    nc.scalar.activation(sqb[:, j % 2, :], zT[:, 2 * j:2 * j + 2, :].rearrange("p a n -> p (a n)"),
                                         ACT.Square).then_inc(y_sq, 1)

            def y_root(g):
                act.wait_ge(y_sum, g + 1)
                b = bank[0 if g < 3 else 6]
                nc.scalar.activation(ystd[:, 2 * g:2 * g + 2], b[:, 0:2], ACT.Sqrt, bias=eps,
                                     scale=1.0 / GW).then_inc(y_std, 1)

            hi(C_OUT1 + 2)
            hi(C_OUT1 + 3)
            act.wait_ge(dtw_ready, 1)
            act.wait_ge(chunk_used, C_OUT1)
            for m in range(4):
                prep_dm(m)
            for q in range(8):
                act.wait_ge(states, 2 * q + 1)
                if q >= 2:
                    act.wait_ge(yoff_done, 2 * (q - 2) + 1)
                    act.wait_ge(h_decayed, q - 1)
                nc.scalar.activation(H0[:, q % 2, :], bank[0][:, :], ACT.Copy).then_inc(h0_ready, 1)
                for m in range(4 * q, 4 * q + 4):
                    act.wait_ge(seg_done, m + 1)
                    if m >= 2:
                        act.wait_ge(m_ready, m - 1)
                    nc.scalar.activation(Eb[:, m % 2, :, :].rearrange("p a n -> p (a n)"), bank[2 + m % 2][:, :],
                                         ACT.Exp).then_inc(e_ready, 1)
                    if q < 7:
                        prep_dm(m + 4)
                if q >= 2 and q % 2 == 0:
                    y_square(q // 2 - 1)
                if q >= 2 and q % 2 == 1:
                    y_root(q // 2 - 1)
            y_square(3)
            y_root(3)
            for g in range(GROUPS):
                act.wait_ge(y_full, g + 1)
                nc.scalar.activation(yhi[:, 4 * g:4 * g + 4, :], zT[:, 4 * g:4 * g + 4, :], ACT.Copy)\
                    .then_inc(y_hi, 1)
            hi(C_OUT1 + 4)
            hi(C_OUT1 + 5)
            for t in range(KT):
                if 1 <= t < KT - 1:
                    hi(C_OUT1 + 2 * t + 4)
                    hi(C_OUT1 + 2 * t + 5)
                act.wait_ge(freed, F_OUT1 + t + 1)
                square(3, t, cols=LAT)
            norm_std(3, (LAT,))
            norm(3, (LAT,))
            for p in range(2):
                ffn_in(1, p)
            with act.Fori(0, 4) as i:
                for p in range(2, 6):
                    ffn_in(1, p, 4, i)
            for p in range(18, FT):
                ffn_in(1, p)
            for c in range(C_FO1, C_END):
                hi(c + 2)

        @block.gpsimd
        def _(gp):
            def prep_x(q):
                g, d = q // 2, q % 2
                if q >= 2:
                    gp.wait_ge(ydiag_done, 4 * (q - 2) + 4)
                    gp.wait_ge(states, 2 * (q - 2) + 2)
                for n in range(3):
                    w = dtW[:, 3 * d + n, g * HPG:(g + 1) * HPG]
                    nc.gpsimd.tensor_tensor(heads(xs_[:, q % 2, n, :]), x_of(SPANS[3 * d + n][1], g), per_head(w), ALU.mult)\
                        .then_inc(x_ready, 1)
                for c2 in range(2):
                    w = dt_[:, 2 + c2, 32 * d + g * HPG:32 * d + (g + 1) * HPG]
                    nc.gpsimd.tensor_tensor(heads(xs_[:, q % 2, 3 + c2, :]), x_of(2 + c2, g), per_head(w), ALU.mult)\
                        .then_inc(x_ready, 1)

            def lo(c, per=0, i=None):
                gp.wait_ge(hi_ready, at(c + 1, per, i))
                w, s = chunk_width(c), c % RING
                nc.gpsimd.tensor_tensor(wlo[:, s, 0:w], raw[:, s, 0:w], whi[:, s, 0:w].bitcast(F32),
                                        ALU.subtract).then_inc(lo_ready, 1)

            for c in range(C_FI0):
                lo(c)
            with gp.Fori(0, FT // 2) as i:
                for k in range(4):
                    lo(C_FI0 + k, 4, i)
            with gp.Fori(0, KT) as i:
                for k in range(4):
                    lo(C_FO0 + k, 4, i)
            with gp.Fori(0, N_IN1 // 4) as i:
                for k in range(4):
                    lo(C_IN1 + k, 4, i)
            for c in range(C_IN1 + N_IN1 // 4 * 4, C_VEC):
                lo(c)
            gp.wait_ge(tok_ready, 20)
            gp.wait_ge(dtw_ready, 1)
            gp.wait_ge(chunk_used, C_OUT1)
            for q in range(8):
                prep_x(q)

        @block.vector
        def _(dve):
            vec = nc.vector

            def lo(c, per=0, i=None):
                if c >= C_END:
                    return
                dve.wait_ge(hi_ready, at(c + 1, per, i))
                w, s = chunk_width(c), c % RING
                vec.tensor_tensor(wlo[:, s, 0:w], raw[:, s, 0:w], whi[:, s, 0:w].bitcast(F32),
                                  ALU.subtract).then_inc(lo_ready, 1)

            def add_bias(dst, src, row, per=0, i=None):
                b = pv[:, bass.ds(at(PV_ADAB + row * KT, per * KT, i), KT)]
                b = b.rearrange("p (a n) -> p a n", n=1).broadcast_to([P, KT, dst.shape[2]])
                return vec.tensor_tensor(dst, src, b, ALU.add)

            def ada_step(a, per=0, i=None):
                t = a % KT
                dve.wait_ge(ada_in[a % 2], at(16 * (a // 2 + 1), 8 * per, i))
                if a:
                    dve.wait_ge(ada_used, at(a, per, i))
                else:
                    dve.wait_ge(crow_silu, 1)
                if t == 0:
                    dve.wait_ge(mods_ready, at(a // KT + 2, per // KT, i))
                lat_only = a >= 8 * U_LAT
                for c in range(1 if lat_only else 0, 2):
                    vec.scalar_tensor_tensor(out=junk[:, :], in0=aring[:, a % 2, :], scalar=1.0,
                                             in1=csil[:, c, :], op0=ALU.mult, op1=ALU.mult,
                                             accum_out=asum[:, t, c:c + 1]).then_inc((ada_half, ada_used)[c], 1)
                    if c == 0:
                        dve.wait_ge(ada_half, at(a + 1, per, i))
                if t == KT - 1:
                    dve.wait_ge(ada_used, at(a + 1, per, i))
                    c = slice(1 if lat_only else 0, 2)
                    row = a // KT + 2
                    dst = mod[:, bass.ds(at(row, per // KT, i), 1)].rearrange("p a k c -> p (a k) c")
                    add_bias(dst[:, :, c], asum[:, :, c], row, per // KT, i).then_inc(mods_ready, 1)

            def gains(k, mods):
                dve.wait_ge(mods_ready, mods)
                g = pv[:, PV_G + k * KT:PV_G + (k + 1) * KT].rearrange("p (a n) -> p a n", n=1)
                c = slice(1 if k == 3 else 0, 2)
                vec.scalar_tensor_tensor(out=gain[:, k, :, c], in0=mod[:, 6 * (k // 2) + 3 * (k % 2) + 1, :, c],
                                         scalar=1.0, in1=g.broadcast_to([P, KT, 2 - c.start]), op0=ALU.add,
                                         op1=ALU.mult)\
                    .then_inc(gains_ready, 1)

            def spread(dst, src):
                a, n = src.shape[1], dst.shape[1] // src.shape[1]
                return vec.tensor_copy(dst.rearrange("p (a n) -> p a n", a=a),
                                       src.rearrange("p (a n) -> p a n", n=1).broadcast_to([P, a, n]))

            def clear_sum(k):
                vec.memset(sqacc[:, :], 0.0).then_inc(sq_added, 1)

            def add_square(k, t, per=0, i=None, cols=ALL):
                dve.wait_ge(squared, at(KT * k + t + 1, per, i))
                dve.wait_ge(sq_added, at(9 * k + t + 1, per, i))
                vec.tensor_tensor(sqacc[:, cols], sqacc[:, cols], sqb[:, t % 2, cols], ALU.add)\
                    .then_inc(sq_added, 1)

            def norm_rstd(k, halves):
                tt0 = halves[0].start // P
                dve.wait_ge(std_ready, k + 1)
                vec.reciprocal(nrst[:, tt0:4], nstd[:, tt0:4]).then_inc(rstd_ready, 1)
                dve.wait_ge(rstd_ready, k + 1)
                spread(scr[:, 2, tt0 * P:T], nrst[:, tt0:4]).then_inc(norm_bc, 1)

            def norm(k, halves):
                shift = 6 * (k // 2) + 3 * (k % 2)
                dve.wait_ge(norm_back, k + 1)
                dve.wait_ge(gains_ready, k + 1)
                for t in range(KT + 1):
                    if t < KT:
                        if t >= 2:
                            dve.wait_ge(hlo_ready, KT * k + t - 1)
                        for h in halves:
                            c = 0 if h is CTX else 1
                            last = vec.scalar_tensor_tensor(out=scr[:, t % 2, h], in0=xT[:, t, h],
                                                            scalar=gain[:, k, t, c:c + 1], in1=bank[7][:, h],
                                                            op0=ALU.mult, op1=ALU.mult)
                        last.then_inc(scaled, 1)
                    if t >= 1:
                        s = t - 1
                        dve.wait_ge(hhi_ready, KT * k + s + 1)
                        for h in halves:
                            c = 0 if h is CTX else 1
                            last = vec.scalar_tensor_tensor(out=hlo[:, s, h], in0=scr[:, s % 2, h],
                                                            scalar=mod[:, shift, s, c:c + 1],
                                                            in1=hhi[:, s, h].bitcast(F32),
                                                            op0=ALU.add, op1=ALU.subtract)
                        last.then_inc(hlo_ready, 1)

            def residual(row, t, b, halves, psum, per=0, i=None):
                for h in halves:
                    c = 0 if h is CTX else 1
                    xt = xT[:, bass.ds(at(t, per, i), 1), h].rearrange("p a n -> p (a n)")
                    g = mod[:, row, bass.ds(at(t, per, i), 1), c]
                    last = vec.scalar_tensor_tensor(out=xt, in0=bank[b][:, psum(h)], scalar=g, in1=xt,
                                                    op0=ALU.mult, op1=ALU.add)
                last.then_inc(freed, 1)

            def ffn_in(l, p, per=0, i=None):
                cbase, fbase = (C_FI0, C_FI1)[l], (F_FI0, F_FI1)[l]
                cols = (ALL, LAT)[l]
                if l == 1:
                    lo(cbase + 2 * p + 2, 2 * per, i)
                    lo(cbase + 2 * p + 3, 2 * per, i)
                elif p >= 2:
                    ada_step(8 * U_FI0 + 2 * p - 4, 2 * per, i)
                    ada_step(8 * U_FI0 + 2 * p - 3, 2 * per, i)
                dve.wait_ge(chunk_used, at(cbase + 2 * p + 2, 2 * per, i))
                dve.wait_ge(silu_ready, at(FT * l + p + 1, per, i))
                if p >= 2:
                    dve.wait_ge(alo_ready, at(FT * l + p - 1, per, i))
                vec.tensor_tensor(scr[:, 2 + p % 2, cols], scr[:, p % 2, cols], bank[2 * (p % 2) + 1][:, cols],
                                  ALU.mult).then_inc(freed, 1)
                dve.wait_ge(ahi_ready, at(FT * l + p + 1, per, i))
                dst = alo[:, bass.ds(at(p, per, i), 1), cols].rearrange("p a n -> p (a n)")
                src = ahi[:, bass.ds(at(p, per, i), 1), cols].rearrange("p a n -> p (a n)")
                vec.tensor_tensor(dst, scr[:, 2 + p % 2, cols], src.bitcast(F32), ALU.subtract)\
                    .then_inc(alo_ready, 1)

            clear_sum(0)
            for t in range(KT):
                add_square(0, t)
            norm_rstd(0, HALVES)
            for n, row in enumerate((1, 0)):
                dve.wait_ge(ada0_sum, n + 1)
                add_bias(mod[:, row], bank[4 + n][:, 0:16].rearrange("p (k c) -> p k c", c=2), row)\
                    .then_inc(mods_ready, 1)
            gains(0, 2)
            norm(0, HALVES)

            n_rst = n_rope = n_scaled = 0
            srcs = {"gv": gvT, "k": kT, "q": qT}
            gcol = {"gv": PV_SG, "k": PV_KG, "q": PV_QG}
            done_at = {}
            for s in range(STEPS0):
                for name, j in ITEMS.get(s - 1, []):
                    n, w = n_rst, 4 if name == "gv" else 8
                    dve.wait_ge(it_std, n + 1)
                    vec.reciprocal(irst[:, n % 2, 0:w], istd[:, n % 2, 0:w]).then_inc(it_rst, 1)
                    dve.wait_ge(it_rst, n + 1)
                    if n >= 2:
                        dve.wait_ge(it_back, n - 1)
                    spread(ibc[:, n % 2, :], irst[:, n % 2, 0:w]).then_inc(it_bc, 1)
                    n_rst += 1
                for name, j in ITEMS.get(s - 2, []):
                    if name == "gv":
                        continue
                    r = n_rope
                    src = srcs[name][:, j, LAT]
                    dve.wait_ge(it_scaled, ORDER.index((name, j)) + 1)
                    if r:
                        dve.wait_ge(roped, r)
                    else:
                        dve.wait_ge(k0_in, 16)
                    vec.tensor_tensor(rtmp[:, 0, :], src, k0[:, A_COS:A_COS + NLAT], ALU.mult)
                    dve.wait_ge(rot_done, r + 1)
                    vec.tensor_tensor(rtmp[:, 1, :], bank[7][:, 0:NLAT], k0[:, A_SIN:A_SIN + NLAT], ALU.mult)\
                        .then_inc(rope_tmp, 1)
                    dve.wait_ge(rope_tmp, r + 1)
                    vec.tensor_tensor(src, rtmp[:, 0, :], rtmp[:, 1, :], ALU.add).then_inc(roped, 1)
                    n_rope += 1
                for name, j in ITEMS.get(s - 1, []):
                    g = gcol[name] + (j if name == "gv" else 0)
                    dve.wait_ge(it_back, n_scaled + 1)
                    vec.scalar_tensor_tensor(out=srcs[name][:, j, :], in0=srcs[name][:, j, :],
                                             scalar=pv[:, g:g + 1], in1=bank[5 + n_scaled % 2][:, :],
                                             op0=ALU.mult, op1=ALU.mult).then_inc(it_scaled, 1)
                    n_scaled += 1
                for a in ADA_AT.get(s, ()):
                    ada_step(a)
            for n in range(39):
                if n < 32:
                    keys = P * key_tiles(UNITS[n][0])
                    dve.wait_ge(scores_ready, n + 1)
                    vec.reduce_max(attn_s[:, n % 4, 0:1], bank[n % 2][:, 0:keys], AX_X).then_inc(rowmax, 1)
                    dve.wait_ge(rowmax, n + 1)
                    vec.tensor_scalar(attn_s[:, n % 4, 1:2], attn_s[:, n % 4, 0:1], -(HD ** -0.5), None, ALU.mult)\
                        .then_inc(bias_ready, 1)
                m = n - 1
                if 0 <= m < 32:
                    keys = P * key_tiles(UNITS[m][0])
                    dve.wait_ge(exp_done, m + 1)
                    vec.reciprocal(attn_s[:, m % 4, 3:4], attn_s[:, m % 4, 2:3]).then_inc(recip_done, 1)
                    dve.wait_ge(recip_done, m + 1)
                    vec.tensor_scalar(prob[:, m % 3, 0:keys], prob[:, m % 3, 0:keys], attn_s[:, m % 4, 3:4], None,
                                      ALU.mult).then_inc(probs_ready, 1)
                if n % 8 == 7 and n < 32:
                    g = n // 8
                    dve.wait_ge(spatial, g + 1)
                    b = k0[:, A_SGB + g * P:A_SGB + (g + 1) * P].rearrange("p (a n) -> p a n", a=1)
                    vec.tensor_tensor(gvT[:, g, :].rearrange("p (a n) -> p a n", n=P),
                                      bank[4][:, :].rearrange("p (a n) -> p a n", n=P),
                                      b.broadcast_to([P, 4, P]), ALU.add).then_inc(sgu_biased, 1)
                if n % 2 == 0 and n <= 20:
                    ada_step(15 + n // 2)
                if n >= 33:
                    g = n - 33
                    if g < GROUPS:
                        dve.wait_ge(u_gelu, g + 1)
                        dve.wait_ge(sgu_biased, GROUPS)
                        vec.tensor_tensor(uT[:, g, :], uT[:, g, :], gvT[:, g, :], ALU.mult).then_inc(sgu_full, 1)
                    if g >= 1 and g - 1 < GROUPS:
                        dve.wait_ge(sgu_hi, g)
                        vec.tensor_tensor(hlo[:, 3 + g, :], uT[:, g - 1, :], hhi[:, 3 + g, :].bitcast(F32),
                                          ALU.subtract).then_inc(sgu_lo, 1)
                if n % 8 == 4 and n >= 12:
                    qb = (n - 12) // 8
                    dve.wait_ge(att_hi, qb + 1)
                    vec.tensor_tensor(hlo[:, 0:4, qb * P:(qb + 1) * P],
                                      bank[5 + qb % 2][:, :].rearrange("p (a n) -> p a n", n=P),
                                      hhi[:, 0:4, qb * P:(qb + 1) * P].bitcast(F32), ALU.subtract)\
                        .then_inc(att_lo, 1)
            clear_sum(1)
            gains(1, 5)
            for t in range(KT):
                dve.wait_ge(chunk_used, C_OUT0 + t + 1)
                dve.wait_ge(mods_ready, 5)
                residual(2, t, t % 2, HALVES, lambda h: h)
                add_square(1, t)
                if t < KT - 2:
                    ada_step(26 + t)
            norm_rstd(1, HALVES)
            norm(1, HALVES)
            for p in range(2):
                ffn_in(0, p)
            with dve.Fori(0, 4) as i:
                for p in range(2, 6):
                    ffn_in(0, p, 4, i)
            for p in range(18, FT):
                ffn_in(0, p)
            clear_sum(2)
            for t in range(KT):
                for k in range(4):
                    if t < 2:
                        ada_step(8 * U_FO0 + 4 * t + k)
                dve.wait_ge(chunk_used, C_FO0 + 4 * t + 4)
                residual(5, t, t % 2, HALVES, lambda h: h)
                add_square(2, t)
            gains(2, 12)
            gains(3, 12)
            norm_rstd(2, HALVES)
            norm(2, HALVES)

            def conv(j, e, per=0, i=None):
                segs = 2 if e < 20 else 1
                c = scr[:, e % 2, 0:256 * segs].rearrange("p (a n) -> p a n", a=segs)
                b = bank[j % 4][:, 0:256 * segs].rearrange("p (a n) -> p a n", a=segs)
                left, _, right = conv_taps(e)
                dve.wait_ge(conv_mid, at(e + 1, per, i))
                vec.scalar_tensor_tensor(out=c[:, :, 1:256], in0=b[:, :, 0:255],
                                         scalar=pv[:, bass.ds(at(left, per, i), 1)], in1=c[:, :, 1:256],
                                         op0=ALU.mult, op1=ALU.add).then_inc(conv_left, 1)
                dve.wait_ge(conv_left, at(e + 1, per, i))
                vec.scalar_tensor_tensor(out=c[:, :, 0:255], in0=b[:, :, 1:256],
                                         scalar=pv[:, bass.ds(at(right, per, i), 1)], in1=c[:, :, 0:255],
                                         op0=ALU.mult, op1=ALU.add).then_inc(freed, 1)
                if e < 4:
                    dve.wait_ge(conv_silu, e + 1)
                    vec.tensor_copy(BT[:, e, :], scr[:, 2 + e % 2, LAT]).then_inc(bt_ready, 1)

            conv(0, 0)
            conv(1, 1)
            dve.wait_ge(chunk_used, C_IN1 + 3)
            vec.tensor_scalar(sqb[:, 0, :], bank[2][:, :], pv[:, PV_DTB:PV_DTB + 1], None, ALU.add)\
                .then_inc(freed, 1)
            conv(3, 2)
            conv(4, 3)
            chain = [0]

            def link(ins):
                chain[0] += 1
                ins.then_inc(dt_chain, 1)
                dve.wait_ge(dt_chain, chain[0])

            V, E, Z, Z2, Q = dts[:, 0, :], dts[:, 2, :], dts[:, 3, :], dts[:, 4, :], dts[:, 5, :]
            dve.wait_ge(dt_turned, 1)
            link(vec.tensor_copy(V.rearrange("p (a n) -> p a n", n=NDT),
                                 bank[6][:, :].rearrange("p (a n) -> p a n", n=P)[:, :, 0:NDT]))
            with dve.Fori(0, 4) as i:
                for k in range(4):
                    conv(5 + k, 4 + k, 4, i)
            for k in range(GROUPS):
                conv(21 + k, 20 + k)
            dve.wait_ge(dt_exp, 3)
            link(vec.tensor_scalar(Q, E, 2.0, None, ALU.add))
            link(vec.reciprocal(Z2, Q))
            link(vec.tensor_tensor(Z, E, Z2, ALU.mult))
            link(vec.tensor_tensor(Z2, Z, Z, ALU.mult))
            link(vec.tensor_scalar(Q, Z2, 1.0 / 17, None, ALU.mult))
            for k in range(7, 0, -1):
                link(vec.scalar_tensor_tensor(out=Q, in0=Q, scalar=1.0 / (2 * k + 1), in1=Z2, op0=ALU.add,
                                              op1=ALU.mult))
            link(vec.scalar_tensor_tensor(out=Q, in0=Q, scalar=1.0, in1=Z, op0=ALU.add, op1=ALU.mult))
            link(vec.tensor_scalar(V, V, 0.0, None, ALU.max))
            link(vec.scalar_tensor_tensor(out=dt_[:, :, :].rearrange("p a n -> p (a n)"), in0=Q, scalar=2.0, in1=V,
                                          op0=ALU.mult, op1=ALU.add))
            link(vec.scalar_tensor_tensor(out=da[:, :, :], in0=dt_[:, :, :], scalar=-1.0,
                                          in1=expa[:, :].rearrange("p (a n) -> p a n", a=1)
                                          .broadcast_to([P, 4, NDT]), op0=ALU.mult, op1=ALU.mult))
            for c2 in range(2):
                dve.wait_ge(cb_done, c2 + 1)
                for d in range(2):
                    m = incl[d].rearrange("p (a n) -> p a n", a=1).broadcast_to([P, GROUPS, P])
                    vec.tensor_tensor(CBm[:, d, c2], bank[5 + c2][:, :].rearrange("p (a n) -> p a n", n=P),
                                      m, ALU.mult).then_inc(cbm_ready, 1)
            dve.wait_ge(decays, 1)
            for n, (d, tt) in enumerate(SPANS):
                last = vec.tensor_tensor(dtW[:, n, :], dt_[:, tt, 32 * d:32 * d + 32],
                                         EX[:, EXW + 32 * n:EXW + 32 * n + 32], ALU.mult)
            last.then_inc(dtw_ready, 1)

            def gate(g):
                for j in (2 * g, 2 * g + 1):
                    dve.wait_ge(y_turned, j + 1)
                    dve.wait_ge(z_ready, 2 * j + 2)
                    zz = zT[:, 2 * j:2 * j + 2, :].rearrange("p a n -> p (a n)")
                    vec.tensor_tensor(zz, bank[j % 2][:, :], zz, ALU.mult).then_inc(gated, 1)

            dve.wait_ge(lo_ready, C_VEC)
            lo(C_OUT1 + 2)
            lo(C_OUT1 + 3)
            for q in range(8):
                g, d = q // 2, q % 2
                dve.wait_ge(h0_ready, q + 1)
                dec = per_head(EX[:, EXD + 32 * d + g * HPG:EXD + 32 * d + (g + 1) * HPG])
                if q >= 2:
                    dve.wait_ge(yoff_done, 2 * (q - 2) + 2)
                vec.tensor_tensor(heads(H1[:, q % 2, :]), heads(H0[:, q % 2, :]), dec, ALU.mult).then_inc(h_decayed, 1)
                dve.wait_ge(h_decayed, q + 1)
                dve.wait_ge(states, 2 * q + 2)
                vec.tensor_tensor(H1[:, q % 2, :], H1[:, q % 2, :], bank[1][:, :], ALU.add).then_inc(h1_ready, 1)
                if q == 0:
                    dve.wait_ge(cbm_ready, 4)
                for m in range(4 * q, 4 * q + 4):
                    c2, half = chunk_of(m)
                    dve.wait_ge(e_ready, m + 1)
                    if m >= 4:
                        dve.wait_ge(ydiag_done, m - 3)
                    cb = CBm[:, d, c2, g, :].rearrange("p (a n) -> p a n", a=1).broadcast_to([P, 4, P])
                    vec.tensor_tensor(Mb[:, m % 4], Eb[:, m % 2], cb, ALU.mult).then_inc(m_ready, 1)
                if q >= 2 and d == 0:
                    gate(g - 1)
                for o in range(2):
                    c2 = o ^ d
                    dve.wait_ge(yoff_done, 2 * q + o + 1)
                    e = per_head(EX[:, EXC + 64 * c2 + 32 * d + g * HPG:EXC + 64 * c2 + 32 * d + (g + 1) * HPG])
                    vec.tensor_tensor(heads(scr[:, 2 * d + c2, :]), heads(bank[4 + o][:, :]), e, ALU.mult)\
                        .then_inc(toff_ready, 1)
                if d == 1:
                    dve.wait_ge(toff_ready, 2 * q + 2)
                    if g:
                        dve.wait_ge(y_sum, g)
                    for c2 in range(2):
                        n = 4 * (2 * g + c2)
                        vec.tensor_tensor(sqb[:, 0, :], scr[:, c2, :], scr[:, 2 + c2, :], ALU.add).then_inc(y_part, 1)
                        dd = per_head(pv[:, PV_D + g * HPG:PV_D + (g + 1) * HPG])
                        vec.tensor_tensor(heads(sqb[:, 1, :]), x_of(2 + c2, g), dd, ALU.mult).then_inc(y_part, 1)
                        dve.wait_ge(y_part, n + 2)
                        vec.tensor_tensor(sqacc[:, :], sqb[:, 0, :], sqb[:, 1, :], ALU.add).then_inc(y_part, 1)
                        dve.wait_ge(y_part, n + 3)
                        dve.wait_ge(ydiag_done, 4 * q + 4)
                        vec.tensor_tensor(tok[:, c2, GW + g * GW:GW + (g + 1) * GW], sqacc[:, :], bank[6 + c2][:, :],
                                          ALU.add).then_inc(y_part, 1)
                    dve.wait_ge(y_part, 8 * g + 8)
            dve.wait_ge(y_std, 3)
            vec.reciprocal(yrst[:, 0:6], ystd[:, 0:6]).then_inc(y_rst, 1)
            dve.wait_ge(y_rst, 1)
            for g in range(3):
                spread(scr[:, g, 0:NLAT], yrst[:, 2 * g:2 * g + 2]).then_inc(y_bc, 1)
            gate(3)
            clear_sum(3)

            def scale_y(g):
                dve.wait_ge(y_back, g + 1)
                for k in range(4 * g, 4 * g + 4):
                    last = vec.scalar_tensor_tensor(out=zT[:, k, :], in0=zT[:, k, :],
                                                    scalar=pv[:, PV_YG + k:PV_YG + k + 1],
                                                    in1=bank[2 + g][:, 0:NLAT], op0=ALU.mult, op1=ALU.mult)
                last.then_inc(y_full, 1)

            def split_y(g):
                dve.wait_ge(y_hi, g + 1)
                vec.tensor_tensor(ylo[:, 4 * g:4 * g + 4, :], zT[:, 4 * g:4 * g + 4, :],
                                  yhi[:, 4 * g:4 * g + 4, :].bitcast(F32), ALU.subtract).then_inc(y_lo, 1)

            scale_y(0)
            scale_y(1)
            split_y(0)
            dve.wait_ge(y_std, 4)
            vec.reciprocal(yrst[:, 6:8], ystd[:, 6:8]).then_inc(y_rst, 1)
            dve.wait_ge(y_rst, 2)
            spread(scr[:, 3, 0:NLAT], yrst[:, 6:8]).then_inc(y_bc, 1)
            scale_y(2)
            split_y(1)
            scale_y(3)
            split_y(2)
            split_y(3)
            lo(C_OUT1 + 4)
            for t in range(KT):
                dve.wait_ge(chunk_used, C_OUT1 + (2 * t + 2 if t else 3))
                residual(8, t, t % 2, (LAT,), lambda h: slice(0, NLAT))
                if 1 <= t < KT - 1:
                    lo(C_OUT1 + 2 * t + 4)
                add_square(3, t, cols=LAT)
                if t < KT - 1:
                    lo(C_OUT1 + 2 * t + 5)
            norm_rstd(3, (LAT,))
            norm(3, (LAT,))
            for p in range(2):
                ffn_in(1, p)
            with dve.Fori(0, 4) as i:
                for p in range(2, 6):
                    ffn_in(1, p, 4, i)
            for p in range(18, FT):
                ffn_in(1, p)
            for t in range(KT):
                for k in range(4):
                    lo(C_FO1 + 4 * t + k + 2)
                dve.wait_ge(chunk_used, C_FO1 + 4 * t + 4)
                residual(11, t, t % 2, (LAT,), lambda h: slice(0, NLAT))

        @block.tensor
        def _(pe):
            mm = nc.tensor.matmul

            def turn(dst, src):
                return nc.tensor.transpose(dst, src, ident)

            def chunk(dst, c, xhi, xlo, k0_, n, first, last, per=0, i=None, ready=None):
                pe.wait_ge(lo_ready, at(c + 1, per, i))
                s = c % RING
                for j in range(n):
                    if ready is not None:
                        pe.wait_ge(ready[0], ready[1] + k0_ + j + 1)
                    for w, xx, o in ((whi, xhi, 0), (whi, xlo, 1), (wlo, xhi, 2)):
                        ins = mm(dst, w[:, s, j * P:(j + 1) * P], xx[:, k0_ + j],
                                 start=first and j == 0 and o == 0, stop=last and j == n - 1 and o == 2)
                ins.then_inc(chunk_used, 1)

            def part_chunk(dst, c, j0, n):
                pe.wait_ge(lo_ready, c + 1)
                for j in range(j0, j0 + n):
                    for w, xx, o in ((whi, hhi, 0), (whi, hlo, 1), (wlo, hhi, 2)):
                        ins = mm(dst, w[:, c % RING, j * P:(j + 1) * P], xx[:, j], start=j == 0 and o == 0,
                                 stop=j == KT - 1 and o == 2)
                if j0 + n == KT:
                    ins.then_inc(chunk_used, 1)

            def two_chunks(dsts, c, xhi, xlo, ready):
                pe.wait_ge(lo_ready, c + 2)
                for j in range(KT):
                    pe.wait_ge(*ready[j])
                    for n, dst in enumerate(dsts):
                        s = (c + n) % RING
                        for w, xx, o in ((whi, xhi, 0), (whi, xlo, 1), (wlo, xhi, 2)):
                            ins = mm(dst, w[:, s, j * P:(j + 1) * P], xx[:, j], start=j == 0 and o == 0,
                                     stop=j == KT - 1 and o == 2)
                        if j == KT - 1:
                            ins.then_inc(chunk_used, 1)

            def norm_total(k, cols):
                tts = range(cols.start // P, cols.stop // P)
                pe.wait_ge(sq_added, 9 * k + 9)
                for tt in tts:
                    ins = mm(bank[7][:, tt:tt + 1], sqacc[:, tt * P:(tt + 1) * P], ones[:, 0:1], start=True, stop=True)
                ins.then_inc(norm_sum, 1)

            def norm_turn(k, cols):
                tts = range(cols.start // P, cols.stop // P)
                pe.wait_ge(norm_bc, k + 1)
                for tt in tts:
                    ins = turn(bank[7][:, tt * P:(tt + 1) * P], scr[:, 2, tt * P:(tt + 1) * P])
                ins.then_inc(norm_back, 1)

            def ffn_in(l, p, per=0, i=None):
                cbase, fbase = (C_FI0, C_FI1)[l], (F_FI0, F_FI1)[l]
                cols = (ALL, LAT)[l]
                pe.wait_ge(freed, at(fbase + p - 1, per, i))
                if p == 0:
                    two_chunks([bank[k][:, cols] for k in range(2)], cbase, hhi[:, :, cols], hlo[:, :, cols],
                               [(hlo_ready, KT * (1 + 2 * l) + k + 1) for k in range(KT)])
                    return
                for k in range(2):
                    chunk(bank[2 * (p % 2) + k][:, cols], cbase + 2 * p + k, hhi[:, :, cols], hlo[:, :, cols], 0, KT,
                          True, True, 2 * per, i)

            def ffn_out(l, t):
                cbase, fbase = (C_FO0, C_FO1)[l], (F_FO0, F_FO1)[l]
                cols, dst = (ALL, LAT)[l], (ALL, slice(0, NLAT))[l]
                if t >= 2:
                    pe.wait_ge(freed, fbase + t - 1)
                else:
                    pe.wait_ge(freed, fbase)
                for k in range(4):
                    ready = (alo_ready, FT * l) if t == 0 else None
                    chunk(bank[t % 2][:, dst], cbase + 4 * t + k, ahi[:, :, cols], alo[:, :, cols], FO_AT[k],
                          FO_KT[k], k == 0, k == 3, ready=ready)

            pe.wait_ge(cond_silu, 1)

            def turn_rows(n):
                pe.wait_ge(rows_out, n + 1)
                for f in range(4):
                    col = 2 * (4 * (n % 2) + f)
                    ins = nc.tensor.transpose(bank[4 + n // 2][:, col:col + 2], rows0[0:2, n, f * P:(f + 1) * P],
                                              kc[0:2, K_ID:K_ID + 2])
                if n % 2:
                    ins.then_inc(ada0_sum, 1)

            for n in range(4):
                pe.wait_ge(ada0_in[n], 16)
                for k in range(KT):
                    ins = mm(bank[n][0:2, :], silc[:, 2 * k:2 * k + 2], ada0[:, n, k, :], start=k == 0,
                             stop=k == KT - 1)
                ins.then_inc(ada0_rows, 1)
                if n == 1:
                    pe.wait_ge(const_in, 16)
                if n:
                    turn_rows(n - 1)
                if n == 2:
                    norm_total(0, ALL)
                if n == 3:
                    norm_turn(0, ALL)
            turn_rows(3)

            n_sum = n_rot = n_back = 0
            srcs = {"gv": gvT, "k": kT, "q": qT}

            def token_sums(n, name):
                pe.wait_ge(it_sq, n + 1)
                if n >= 2:
                    pe.wait_ge(it_scaled, n - 1)
                if name == "k":
                    pe.wait_ge(k0_in, 16)
                w = ones[:, 0:1] if name == "gv" else k0[:, A_BLK:A_BLK + P:HD]
                heads = w.shape[1]
                for tt in range(4):
                    ins = mm(bank[5 + n % 2][:, heads * tt:heads * (tt + 1)], isq[:, n % 2, tt * P:(tt + 1) * P], w,
                             start=True, stop=True)
                ins.then_inc(it_sum, 1)

            def rotate(n, name, j):
                pe.wait_ge(it_scaled, ORDER.index((name, j)) + 1)
                if n:
                    pe.wait_ge(roped, n)
                mm(bank[7][:, 0:NLAT], k0[:, A_ROT:A_ROT + P], srcs[name][:, j, LAT], start=True, stop=True)\
                    .then_inc(rot_done, 1)

            def turn_tokens(j):
                pe.wait_ge(in0_out, N_DENSE)
                if j >= 2:
                    pe.wait_ge(toks_ready, j - 1)
                if j:
                    pe.wait_ge(it_scaled, ORDER.index(("gv", j - 1)) + 1)
                for tt in range(4):
                    src = vT[:, tt * P:(tt + 1) * P] if j == 0 else gvT[:, j - 1, tt * P:(tt + 1) * P]
                    ins = turn(bank[3 - j % 2][:, tt * P:(tt + 1) * P], src)
                ins.then_inc(turned, 1)

            for s in range(STEPS0):
                if s == 0:
                    pe.wait_ge(rows_out, 4)
                    two_chunks([bank[0][:, :], bank[1][:, :]], C_IN0, hhi, hlo,
                               [(hlo_ready, k + 1) for k in range(KT)])
                elif 2 <= s < N_DENSE:
                    if s >= 4:
                        pe.wait_ge(in0_out, s - 3)
                    part_chunk(bank[s % 4][:, :], s, 0, 4)
                for name, j in ITEMS.get(s - 1, []):
                    token_sums(n_sum, name)
                    n_sum += 1
                for name, j in ITEMS.get(s - 2, []):
                    if name != "gv":
                        rotate(n_rot, name, j)
                        n_rot += 1
                if 2 <= s < N_DENSE:
                    part_chunk(bank[s % 4][:, :], s, 4, 4)
                for _ in ITEMS.get(s - 1, []):
                    n = n_back
                    pe.wait_ge(it_bc, n + 1)
                    for tt in range(4):
                        ins = turn(bank[5 + n % 2][:, tt * P:(tt + 1) * P], ibc[:, n % 2, tt * P:(tt + 1) * P])
                    ins.then_inc(it_back, 1)
                    n_back += 1
            for j in range(5):
                turn_tokens(j)
            for n in range(37):
                if n < 32:
                    qb, kv, i = UNITS[n]
                    keys, rows = P * key_tiles(qb), slice(kv * HD, (kv + 1) * HD)
                    if n == 0:
                        pe.wait_ge(roped, len(ROPED))
                        pe.wait_ge(toks_ready, 5)
                    if n >= 2:
                        pe.wait_ge(exp_done, n - 1)
                    mm(bank[n % 2][:, 0:keys], qT[rows, i, qb * P:(qb + 1) * P], kT[rows, 0, 0:keys],
                       start=True, stop=True).then_inc(scores_ready, 1)
                if n < 12:
                    c = N_DENSE + n // 4
                    if n == 8:
                        pe.wait_ge(in0_out, c - 1)
                    part_chunk(bank[(7, 6, 7)[n // 4]][:, :], c, 2 * (n % 4), 2)
                m = n - 2
                if 0 <= m < 32:
                    pe.wait_ge(probs_ready, m + 1)
                    if m >= 2:
                        pe.wait_ge(probT_ready, m - 1)
                    for tt in range(key_tiles(UNITS[m][0])):
                        ins = turn(bank[2 + m % 2][:, tt * P:(tt + 1) * P], prob[:, m % 3, tt * P:(tt + 1) * P])
                    ins.then_inc(probs_turned, 1)
                if n >= 7 and n % 4 == 3:
                    grp = n // 4 - 1
                    qb, kv, _ = UNITS[4 * grp]
                    rows, kts = slice(kv * HD, (kv + 1) * HD), key_tiles(qb)
                    pe.wait_ge(probT_ready, 4 * grp + 4)
                    if grp == 2:
                        pe.wait_ge(in0_out, N_DENSE + 2)
                    if qb >= 2:
                        pe.wait_ge(att_lo, qb - 1)
                    for tt in range(kts):
                        ins = mm(bank[5 + qb % 2][rows, :], toks[:, 0, tt, kv * HD:(kv + 1) * HD],
                                 probT[:, grp % 2, tt, :, :].rearrange("p a n -> p (a n)"),
                                 start=tt == 0, stop=tt == kts - 1)
                    ins.then_inc(pv_done, 1)
                if n % 8 == 6 and n < 32:
                    g = n // 8
                    if g:
                        pe.wait_ge(sgu_biased, g)
                    for tt in range(4):
                        w = k0[:, A_SGW + g * P:A_SGW + (g + 1) * P]
                        ins = mm(bank[4][:, tt * P:(tt + 1) * P], toks[:, 1 + g, tt, :], w, start=True, stop=True)
                    ins.then_inc(spatial, 1)
            for t in range(KT):
                if t == 0:
                    two_chunks([bank[0][:, :], bank[1][:, :]], C_OUT0, hhi, hlo,
                               [(att_lo, 4)] * 4 + [(sgu_lo, g + 1) for g in range(GROUPS)])
                elif t >= 2:
                    pe.wait_ge(freed, F_OUT0 + t - 1)
                    chunk(bank[t % 2][:, :], C_OUT0 + t, hhi, hlo, 0, KT, True, True)
            norm_total(1, ALL)
            norm_turn(1, ALL)
            for p in range(2):
                ffn_in(0, p)
            with pe.Fori(0, 4) as i:
                for p in range(2, 6):
                    ffn_in(0, p, 4, i)
            for p in range(18, FT):
                ffn_in(0, p)
            for t in range(KT):
                ffn_out(0, t)
            norm_total(2, ALL)
            norm_turn(2, ALL)

            def project(j, cols, per=0, i=None):
                if 4 <= j < 29:
                    pe.wait_ge(freed, at(F_IN1 + j - 3, per, i))
                elif j >= 29:
                    pe.wait_ge(z_ready, j - 28)
                n = cols.stop - cols.start
                chunk(bank[j % 4][:, 0:n], C_IN1 + j, hhi[:, :, cols], hlo[:, :, cols], 0, KT, True, True, per, i)

            def turn_conv(e, per=0, i=None):
                pe.wait_ge(conv_silu, at(e + 1, per, i))
                if e >= 2:
                    pe.wait_ge(tok_ready, at(e - 1, per, i))
                for tt in range(4):
                    ins = turn(bank[4 + e % 2][:, tt * P:(tt + 1) * P], scr[:, 2 + e % 2, tt * P:(tt + 1) * P])
                ins.then_inc(conv_turned, 1)

            two_chunks([bank[0][:, :], bank[1][:, :]], C_IN1, hhi, hlo,
                       [(hlo_ready, 2 * KT + k + 1) for k in range(KT)])
            turn_conv(0)
            project(2, ALL)
            project(3, ALL)
            turn_conv(1)
            pe.wait_ge(freed, F_IN1 + 3)
            for tt in range(4):
                ins = turn(bank[6][:, tt * P:(tt + 1) * P], sqb[:, 0, tt * P:(tt + 1) * P])
            ins.then_inc(dt_turned, 1)
            project(4, ALL)
            turn_conv(2)
            with pe.Fori(0, 4) as i:
                for k in range(4):
                    project(5 + k, ALL, 4, i)
                    turn_conv(3 + k, 4, i)
            for k in range(GROUPS):
                project(21 + k, LAT)
                if k == 0:
                    turn_conv(19)
            for k in range(ZT):
                project(25 + k, LAT)
                if k == 0:
                    pe.wait_ge(conv_silu, 24)
                    pe.wait_ge(bt_ready, GROUPS)
                    pe.wait_ge(tok_ready, 20)
                    pe.wait_ge(dt_chain, 1)
                    for c2 in range(2):
                        for g in range(GROUPS):
                            ins = mm(bank[5 + c2][:, g * P:(g + 1) * P], BT[:, g, c2 * P:(c2 + 1) * P],
                                     CT[:, g, c2 * P:(c2 + 1) * P], start=True, stop=True)
                        ins.then_inc(cb_done, 1)
                if k == 9:
                    pe.wait_ge(dt_chain, 17)
                    for c2 in range(2):
                        for d in range(2):
                            col = EXC + 64 * c2 + 32 * d
                            mm(bank[7][:, col:col + 32], incl[d], da[:, 2 + c2, 32 * d:32 * d + 32], start=True, stop=True)
                    for n, (d, tt) in enumerate(SPANS):
                        rest = {(0, 0): 1, (1, 1): 0}.get((d, tt))
                        col = EXW + 32 * n
                        mm(bank[7][:, col:col + 32], strict[d], da[:, tt, 32 * d:32 * d + 32], start=True, stop=rest is None)
                        if rest is not None:
                            mm(bank[7][:, col:col + 32], ones, da[:, rest, 32 * d:32 * d + 32], start=False, stop=True)
                    for d in range(2):
                        col = EXD + 32 * d
                        ins = mm(bank[7][:, col:col + 32], ones, da[:, 2 + d, 32 * d:32 * d + 32], start=True, stop=True)
                    ins.then_inc(sums_done, 1)

            pe.wait_ge(z_ready, ZT)
            pe.wait_ge(cbm_ready, 4)

            def seg(m):
                pe.wait_ge(dm_ready, m + 1)
                if m >= 2:
                    pe.wait_ge(e_ready, m - 1)
                mm(bank[2 + m % 2][:, :], strict[(m // 4) % 2], DM[:, m % 4].rearrange("p a n -> p (a n)"),
                   start=True, stop=True).then_inc(seg_done, 1)

            def ydiag(m):
                q, i = m // 4, m % 4
                c2, half = (i // 2) ^ (q % 2), i % 2
                pe.wait_ge(m_ready, m + 1)
                if q >= 2 and q % 2 == 0:
                    pe.wait_ge(y_part, 4 * q)
                for hh in range(4):
                    col = (4 * half + hh) * HD
                    ins = mm(bank[6 + c2][:, col:col + HD], Mb[:, m % 4, hh, :], xs_[:, q % 2, 3 + c2, col:col + HD],
                             start=q % 2 == 0 and half == 0 and hh == 0, stop=q % 2 == 1 and half == 1 and hh == 3,
                             skip_group_check=True)
                ins.then_inc(ydiag_done, 1)

            def turn_y(j):
                pe.wait_ge(y_part, 8 * (j // 2) + 8)
                for k in range(2):
                    for c2 in range(2):
                        f = GW + (2 * j + k) * P
                        ins = turn(bank[j % 2][:, k * NLAT + c2 * P:k * NLAT + (c2 + 1) * P], tok[:, c2, f:f + P])
                ins.then_inc(y_turned, 1)

            def total_y(g):
                pe.wait_ge(y_sq, 2 * g + 2)
                b = bank[0 if g < 3 else 6]
                for c2 in range(2):
                    for k in range(4):
                        col = (k % 2) * NLAT + c2 * P
                        ins = mm(b[:, c2:c2 + 1], sqb[:, k // 2, col:col + P], ones[:, 0:1], start=k == 0, stop=k == 3)
                ins.then_inc(y_sum, 1)

            for q in range(8):
                g, d = q // 2, q % 2
                b_tok = tok[:, :, g * P:(g + 1) * P]
                if q:
                    pe.wait_ge(h0_ready, q)
                    pe.wait_ge(h1_ready, q)
                if q >= 3:
                    pe.wait_ge(gated, 2 * ((q - 1) // 2))
                if q >= 4 and q % 2 == 0:
                    pe.wait_ge(y_std, q // 2 - 1)
                pe.wait_ge(x_ready, 5 * q + 2)
                for tt in range(2):
                    ins = mm(bank[0][:, :], b_tok[:, tt, :], xs_[:, q % 2, tt, :], start=tt == 0, stop=tt == 1)
                ins.then_inc(states, 1)
                pe.wait_ge(x_ready, 5 * q + 5)
                mm(bank[1][:, :], b_tok[:, 2 + d, :], xs_[:, q % 2, 2, :], start=True, stop=True).then_inc(states, 1)
                seg(4 * q)
                seg(4 * q + 1)
                for o in range(2):
                    c2 = o ^ d
                    if o == 0:
                        pe.wait_ge(h0_ready, q + 1)
                    else:
                        seg(4 * q + 2)
                        ydiag(4 * q)
                        seg(4 * q + 3)
                        ydiag(4 * q + 1)
                        pe.wait_ge(h1_ready, q + 1)
                    if q:
                        pe.wait_ge(toff_ready, 2 * (q - 1) + o + 1)
                    mm(bank[4 + o][:, :], CT[:, g, c2 * P:(c2 + 1) * P], (H0, H1)[o][:, q % 2, :], start=True,
                       stop=True).then_inc(yoff_done, 1)
                    if q >= 2 and d == 0:
                        turn_y(2 * (g - 1) + o)
                if q >= 2 and d == 1:
                    total_y(g - 1)
                ydiag(4 * q + 2)
                ydiag(4 * q + 3)
            pe.wait_ge(y_std, 3)
            turn_y(6)
            turn_y(7)

            def norm_y(g):
                pe.wait_ge(y_bc, g + 1)
                for c2 in range(2):
                    ins = turn(bank[2 + g][:, c2 * P:(c2 + 1) * P], scr[:, g, c2 * P:(c2 + 1) * P])
                ins.then_inc(y_back, 1)

            for g in range(3):
                norm_y(g)
            total_y(3)
            for g in range(GROUPS):
                pe.wait_ge(y_lo, g + 1)
                for t in range(2):
                    c = C_OUT1 + 2 * (g // 2) + t
                    pe.wait_ge(lo_ready, c + 1)
                    for j in range(4 * (g % 2), 4 * (g % 2) + 4):
                        for w, xx, o in ((whi, yhi, 0), (whi, ylo, 1), (wlo, yhi, 2)):
                            ins = mm(bank[t][:, 0:NLAT], w[:, c % RING, j * P:(j + 1) * P],
                                     xx[:, KT * (g // 2) + j], start=g == 0 and j == 0 and o == 0,
                                     stop=g == 3 and j == KT - 1 and o == 2)
                    if g % 2:
                        ins.then_inc(chunk_used, 1)
                if g == 0:
                    norm_y(3)
            for t in range(2, KT):
                pe.wait_ge(freed, F_OUT1 + t - 1)
                for k in range(2):
                    chunk(bank[t % 2][:, 0:NLAT], C_OUT1 + 2 * t + k, yhi, ylo, KT * k, KT, k == 0, k == 1)
            norm_total(3, LAT)
            norm_turn(3, LAT)
            for p in range(2):
                ffn_in(1, p)
            with pe.Fori(0, 4) as i:
                for p in range(2, 6):
                    ffn_in(1, p, 4, i)
            for p in range(18, FT):
                ffn_in(1, p)
            for t in range(KT):
                ffn_out(1, t)


def tiles(w, k_per=KT):
    k, n = w.shape
    w = w.reshape(k // P, P, n // P, P).transpose(2, 1, 0, 3).reshape(n // P, P, k // P, P)
    w = w.reshape(n // P, P, k // P // k_per, k_per * P).transpose(0, 2, 1, 3)
    return np.ascontiguousarray(w.reshape(-1, P, k_per * P))


def columns(v):
    return v.reshape(-1, P).T


def constants():
    f = np.float32
    t = np.arange(P)
    k = np.concatenate([np.eye(P), np.ones((P, P)), t[:, None] <= t, t[:, None] >= t, t[:, None] > t,
                        t[:, None] < t], axis=1).astype(f)
    tt = np.arange(NLAT)
    inv = f(10000.0) ** (-np.arange(HD // 4, dtype=f) / f(HD // 4))
    ang = np.concatenate([(tt // 64).astype(f)[:, None] * inv, (tt % 64).astype(f)[:, None] * inv], axis=1)
    cos, sin = (np.tile(fn(ang).astype(f).T, (4, 1)) for fn in (np.cos, np.sin))
    rot = np.zeros((P, P), f)
    for j in range(P):
        if j % HD < HD // 2:
            rot[j + HD // 2, j] = -1
        else:
            rot[j - HD // 2, j] = 1
    blk = (t[:, None] // HD == t // HD).astype(f)
    return k, np.concatenate([cos, sin, rot, blk], axis=1)


def kernel(**inputs):
    import concourse.bacc as bacc
    from concourse.bass_utils import run_bass_kernel_spmd

    a = {k: np.asarray(v) for k, v in inputs.items()}
    cat = np.concatenate
    k, k0 = constants()
    sgw = a["sgu_w"][0].transpose(2, 0, 1).reshape(P, GROUPS * P)
    k0 = cat([k0, sgw, np.tile(a["sgu_b"].reshape(1, -1), (P, 1))], axis=1)
    perm = cat([np.arange(h * HD, (h + 1) * HD) for i in range(4) for h in (i, i + 4)])
    w = a["mix_w_in"][0]
    w_in0 = tiles(cat([w[:, 1280:1792], w[:, 512:640], w[:, 640:768], w[:, :512][:, perm], w[:, 768:1280]], axis=1))
    w = a["mix_w_out"][0]
    w_out0 = tiles(cat([w[:512][perm], w[512:]], axis=0))
    w_fi = []
    for l in range(2):
        t = tiles(a["ffn_w_in"][l])
        w_fi.append(np.stack([t[:FT], t[FT:]], axis=1).reshape(2 * FT, P, CW))
    w_fi = cat(w_fi)
    w_fo = cat([tiles(a["ffn_w_out"][l], FT) for l in range(2)])
    w = a["ssm_w_in"][0]
    z, x, b, c, dt = (w[:, s] for s in (slice(0, 2048), slice(2048, 4096), slice(4096, 4608), slice(4608, 5120),
                                        slice(5120, 5184)))
    w_in1 = tiles(cat([b[:, :256], dt, dt, b[:, 256:], x, c, z], axis=1))
    w_out1 = tiles(a["ssm_w_out"][0])
    w_out1 = cat([w_out1[[0, 2, 1, 3]], w_out1[4:]], axis=0)
    ada_w = np.ascontiguousarray(a["ada_w"].reshape(2, D, 6, D).transpose(0, 2, 1, 3).reshape(12, D, D))
    ada_t = np.ascontiguousarray(ada_w[2:].transpose(0, 2, 1)).reshape(10 * KT, P, D)
    ada_w = ada_w[:2]
    crow = np.tile(cat([a["c_ctx"].reshape(1, D), a["c"].reshape(1, D)], axis=1), (P, 1)).reshape(P, 2, D)
    cond = np.stack([a["c_ctx"].reshape(-1), a["c"].reshape(-1)], axis=1).reshape(KT, P, 2)
    norms = cat([a["norm1_g"][0], a["norm2_g"][0], a["norm1_g"][1], a["norm2_g"][1]])
    order = cat([np.arange(16, 20), np.arange(16), np.arange(20, 24)])
    pvec = cat([cond.transpose(1, 0, 2).reshape(P, 2 * KT), columns(a["ada_b"].reshape(-1)), columns(norms),
                np.tile(a["q_norm_g"][0], 2)[:, None], np.tile(a["k_norm_g"][0], 2)[:, None],
                columns(a["sgu_norm_g"][0]),
                *(columns(a["ssm_conv_w"][0, tap])[:, order] for tap in range(3)),
                columns(a["ssm_conv_b"][0])[:, order],
                np.tile(a["ssm_dt_bias"].reshape(-1), 2)[:, None], columns(a["ssm_norm_g"][0]),
                np.tile(a["ssm_a_log"].reshape(1, -1), (P, 1)), np.tile(a["ssm_d"].reshape(1, -1), (P, 1)),
                np.full((P, 1), EPS, np.float32)], axis=1)
    x_in = cat([a["ctx"][0], a["x"][0]], axis=0).T.reshape(KT, P, T).transpose(1, 0, 2)
    arrays = {"x_in": x_in, "consts": k, "consts0": k0, "pvec": pvec, "crow": crow, "ada_w": ada_w, "ada_t": ada_t,
              "w_in0": w_in0,
              "w_out0": w_out0, "w_fi": w_fi, "w_fo": w_fo, "w_in1": w_in1, "w_out1": w_out1}
    arrays = {n: np.ascontiguousarray(v) for n, v in arrays.items()}
    nc = bacc.Bacc("TRN2", target_bir_lowering=False, num_devices=1)
    args = [nc.dram_tensor(f"in_{n}", v.shape, mybir.dt.from_np(v.dtype), kind="ExternalInput").ap()
            for n, v in arrays.items()]
    out = nc.dram_tensor("out_x", (KT, P, NLAT), F32, kind="ExternalOutput").ap()
    build(nc, *args, out)
    r = run_bass_kernel_spmd(nc, [{f"in_{n}": v for n, v in arrays.items()}], core_ids=[0])
    got = r.results[0]["out_x"]
    return np.ascontiguousarray(got.transpose(2, 0, 1).reshape(1, NLAT, D))
```
